# Optimizing a Trainium2 kernel written in Bass

```python
import math
import jax
import jax.numpy as jnp
from jax import lax
import numpy as np

D_MODEL = 1024
BATCH = 1
SEQ = 512
DEPTH = 1

N_HEADS_A = 8
HEAD_DIM = 64
WIDTH_A = N_HEADS_A * HEAD_DIM
KV_RANK = 128
IDX_HEADS = 8
IDX_DIM = 64
TOPK_MAX = 256
N_HEADS_B = 8
WIDTH_B = N_HEADS_B * HEAD_DIM
BLOCK_Q = 128
N_BUCKETS = 32
MAX_EXACT = N_BUCKETS // 2
MAX_DISTANCE = 128
ATTN_SCALE = HEAD_DIM ** -0.5
IDX_SCALE = (IDX_HEADS ** -0.5) * (IDX_DIM ** -0.5)
N_GROUPS = 4
EXPERTS_PER_GROUP = 8
N_EXPERTS = N_GROUPS * EXPERTS_PER_GROUP
D_EXPERT = 256
TOP_K_INNER = 2
PLE_DIM = 256
EPS = 1e-6

_COLS = [
    ("q_a", WIDTH_A),
    ("c_kv", KV_RANK),
    ("q_idx", IDX_HEADS * IDX_DIM),
    ("k_idx", IDX_DIM),
    ("w_idx", IDX_HEADS),
    ("qkv_b", 3 * WIDTH_B),
    ("gate_a", D_MODEL),
    ("gate_b", D_MODEL),
]
IN_COLS = sum(c for _, c in _COLS)


def _rmsnorm(x, g):
    xf = x.astype(jnp.float32)
    y = xf * lax.rsqrt(jnp.mean(xf * xf, axis=-1, keepdims=True) + EPS)
    return (y * g.astype(jnp.float32)).astype(x.dtype)

def _split_cols(proj):
    out = []
    start = 0
    for _, width in _COLS:
        out.append(proj[..., start:start + width])
        start += width
    return out

def _t5_bucket(dist):
    dist = jnp.maximum(dist, 0)
    d_f = jnp.maximum(dist, 1).astype(jnp.float32)
    large = MAX_EXACT + (jnp.log(d_f / MAX_EXACT) / math.log(MAX_DISTANCE / MAX_EXACT)
                         * (N_BUCKETS - MAX_EXACT)).astype(jnp.int32)
    large = jnp.minimum(large, N_BUCKETS - 1)
    return jnp.where(dist < MAX_EXACT, dist, large)

def _dsa_branch(q, c_kv, q_idx, k_idx, w_idx, w_uk, w_uv, rel_bias):
    b, s = q.shape[0], q.shape[1]
    n_sel = min(TOPK_MAX, s // 4)
    n_blocks = s // BLOCK_Q
    q_abs = jnp.einsum("bshd,hcd->bshc", q, w_uk)
    key_pos = jnp.arange(s, dtype=jnp.int32)
    gather = jax.vmap(lambda c, i: c[i])

    def block(i):
        start = i * BLOCK_Q
        t = start + jnp.arange(BLOCK_Q, dtype=jnp.int32)
        qa = lax.dynamic_slice_in_dim(q_abs, start, BLOCK_Q, axis=1)
        qi = lax.dynamic_slice_in_dim(q_idx, start, BLOCK_Q, axis=1)
        wi = lax.dynamic_slice_in_dim(w_idx, start, BLOCK_Q, axis=1).astype(jnp.float32)
        rel = jax.nn.relu(jnp.einsum("bqhe,bse->bqhs", qi, k_idx).astype(jnp.float32))
        score = jnp.einsum("bqhs,bqh->bqs", rel, wi)
        causal = key_pos[None, :] <= t[:, None]
        score = jnp.where(causal[None], score, -jnp.inf)
        _, idx = lax.top_k(score, n_sel)
        valid = idx <= t[None, :, None]
        c_sel = gather(c_kv, idx)
        logits = jnp.einsum("bqhc,bqkc->bhqk", qa, c_sel).astype(jnp.float32) * ATTN_SCALE
        bias = rel_bias[_t5_bucket(t[None, :, None] - idx)]
        logits = logits + jnp.transpose(bias, (0, 3, 1, 2)).astype(jnp.float32)
        logits = jnp.where(valid[:, None], logits, -jnp.inf)
        probs = jax.nn.softmax(logits, axis=-1).astype(c_sel.dtype)
        return jnp.einsum("bhqk,bqkc->bqhc", probs, c_sel)

    o = lax.map(block, jnp.arange(n_blocks, dtype=jnp.int32))
    o = jnp.moveaxis(o, 0, 1).reshape(b, s, N_HEADS_A, KV_RANK)
    return jnp.einsum("bshc,hcd->bshd", o, w_uv)

def _stick_breaking_branch(q, k, v):
    b, s = q.shape[0], q.shape[1]
    n_blocks = s // BLOCK_Q
    key_pos = jnp.arange(s, dtype=jnp.int32)

    def block(i):
        start = i * BLOCK_Q
        t = start + jnp.arange(BLOCK_Q, dtype=jnp.int32)
        qb = lax.dynamic_slice_in_dim(q, start, BLOCK_Q, axis=1)
        z = jnp.einsum("bqhd,bshd->bhqs", qb, k).astype(jnp.float32) * ATTN_SCALE
        mask = (key_pos[None, :] < t[:, None])[None, None]
        log_1m = jnp.where(mask, jax.nn.log_sigmoid(-z), 0.0)
        after = lax.cumsum(log_1m, axis=3, reverse=True) - log_1m
        log_a = jax.nn.log_sigmoid(z) + after
        a = jnp.where(mask, jnp.exp(log_a), 0.0).astype(v.dtype)
        return jnp.einsum("bhqs,bshd->bqhd", a, v)

    o = lax.map(block, jnp.arange(n_blocks, dtype=jnp.int32))
    return jnp.moveaxis(o, 0, 1).reshape(b, s, N_HEADS_B, HEAD_DIM)

def _hier_moe(h, w_r1, b_r1, w_r2, b_r2, w_gate, w_up, w_down):
    b, s, d = h.shape
    hf = h.reshape(b * s, d)
    n_tok = b * s
    g_logits = jnp.matmul(hf, w_r1).astype(jnp.float32) + b_r1.astype(jnp.float32)
    g_prob = jax.nn.softmax(g_logits, axis=-1)
    g_sel = jnp.argmax(g_logits, axis=-1)
    p_g = jnp.take_along_axis(g_prob, g_sel[:, None], axis=1)[:, 0]
    e_logits = jnp.einsum("nd,gde->nge", hf, w_r2).astype(jnp.float32) + b_r2.astype(jnp.float32)
    e_sel = jnp.take_along_axis(e_logits, g_sel[:, None, None], axis=1)[:, 0]
    top_v, top_i = lax.top_k(e_sel, TOP_K_INNER)
    w_inner = jax.nn.softmax(top_v, axis=-1)
    inner = jnp.sum(jax.nn.one_hot(top_i, EXPERTS_PER_GROUP, dtype=jnp.float32) * w_inner[..., None], axis=1)
    comb = (jax.nn.one_hot(g_sel, N_GROUPS, dtype=jnp.float32)[:, :, None]
            * inner[:, None, :] * p_g[:, None, None])
    comb = comb.reshape(n_tok, N_EXPERTS).astype(h.dtype)
    out = jnp.zeros_like(hf)
    for e in range(N_EXPERTS):
        hid = jax.nn.silu(jnp.matmul(hf, w_gate[e])) * jnp.matmul(hf, w_up[e])
        out = out + comb[:, e:e + 1] * jnp.matmul(hid, w_down[e])
    return out.reshape(b, s, d)

def first_inputs(seed: int = 0) -> dict:
    key = jax.random.key(seed)
    ks = jax.random.split(key, 24)
    f32 = jnp.float32

    def nrm(k, shape, fan_in):
        return jax.random.normal(k, shape, f32) * (fan_in ** -0.5)

    def gain(k, shape):
        return 1.0 + 0.05 * jax.random.normal(k, shape, f32)

    return {
        "x": jax.random.normal(ks[0], (BATCH, SEQ, D_MODEL), f32),
        "p": jax.random.normal(ks[1], (DEPTH, BATCH, SEQ, PLE_DIM), f32),
        "attn_norm": gain(ks[2], (DEPTH, D_MODEL)),
        "w_in": nrm(ks[3], (DEPTH, D_MODEL, IN_COLS), D_MODEL),
        "kv_norm": gain(ks[4], (DEPTH, KV_RANK)),
        "w_uk": nrm(ks[5], (DEPTH, N_HEADS_A, KV_RANK, HEAD_DIM), KV_RANK),
        "w_uv": nrm(ks[6], (DEPTH, N_HEADS_A, KV_RANK, HEAD_DIM), KV_RANK),
        "rel_bias": 0.5 * jax.random.normal(ks[7], (N_BUCKETS, N_HEADS_A), f32),
        "w_branch_a": nrm(ks[8], (DEPTH, WIDTH_A, D_MODEL), WIDTH_A),
        "w_branch_b": nrm(ks[9], (DEPTH, WIDTH_B, D_MODEL), WIDTH_B),
        "w_out": nrm(ks[10], (DEPTH, D_MODEL, D_MODEL), D_MODEL),
        "ffn_norm": gain(ks[11], (DEPTH, D_MODEL)),
        "w_r1": nrm(ks[12], (DEPTH, D_MODEL, N_GROUPS), D_MODEL),
        "b_r1": 0.01 * jax.random.normal(ks[13], (DEPTH, N_GROUPS), f32),
        "w_r2": nrm(ks[14], (DEPTH, N_GROUPS, D_MODEL, EXPERTS_PER_GROUP), D_MODEL),
        "b_r2": 0.01 * jax.random.normal(ks[15], (DEPTH, N_GROUPS, EXPERTS_PER_GROUP), f32),
        "w_gate": nrm(ks[16], (DEPTH, N_EXPERTS, D_MODEL, D_EXPERT), D_MODEL),
        "w_up": nrm(ks[17], (DEPTH, N_EXPERTS, D_MODEL, D_EXPERT), D_MODEL),
        "w_down": nrm(ks[18], (DEPTH, N_EXPERTS, D_EXPERT, D_MODEL), D_EXPERT),
        "ple_norm": gain(ks[19], (DEPTH, D_MODEL)),
        "w_ple_gate": nrm(ks[20], (DEPTH, D_MODEL, D_MODEL), D_MODEL),
        "w_ple": nrm(ks[21], (DEPTH, PLE_DIM, D_MODEL), PLE_DIM),
        "final_norm": gain(ks[22], (D_MODEL,)),
    }

def first_block(x, p, attn_norm, w_in, kv_norm, w_uk, w_uv, rel_bias, w_branch_a, w_branch_b,
              w_out, ffn_norm, w_r1, b_r1, w_r2, b_r2, w_gate, w_up, w_down,
              ple_norm, w_ple_gate, w_ple, final_norm):
    b, s, _ = x.shape
    for i in range(DEPTH):
        h = _rmsnorm(x, attn_norm[i])
        proj = jnp.matmul(h, w_in[i])
        q_a, c_kv, q_idx, k_idx, w_idx, qkv_b, gate_a, gate_b = _split_cols(proj)
        q_a = q_a.reshape(b, s, N_HEADS_A, HEAD_DIM)
        c_kv = _rmsnorm(c_kv, kv_norm[i])
        q_idx = q_idx.reshape(b, s, IDX_HEADS, IDX_DIM)
        w_idx = w_idx * IDX_SCALE
        q_b, k_b, v_b = jnp.split(qkv_b.reshape(b, s, 3, N_HEADS_B, HEAD_DIM), 3, axis=2)
        o_a = _dsa_branch(q_a, c_kv, q_idx, k_idx, w_idx, w_uk[i], w_uv[i], rel_bias)
        o_b = _stick_breaking_branch(q_b[:, :, 0], k_b[:, :, 0], v_b[:, :, 0])
        y_a = jnp.matmul(o_a.reshape(b, s, WIDTH_A), w_branch_a[i])
        y_b = jnp.matmul(o_b.reshape(b, s, WIDTH_B), w_branch_b[i])
        merged = jax.nn.sigmoid(gate_a) * y_a + jax.nn.sigmoid(gate_b) * y_b
        x = x + jnp.matmul(merged, w_out[i])
        h2 = _rmsnorm(x, ffn_norm[i])
        x = x + _hier_moe(h2, w_r1[i], b_r1[i], w_r2[i], b_r2[i], w_gate[i], w_up[i], w_down[i])
        h3 = _rmsnorm(x, ple_norm[i])
        x = x + jnp.matmul(p[i], w_ple[i]) * jax.nn.sigmoid(jnp.matmul(h3, w_ple_gate[i]))
    return _rmsnorm(x, final_norm)


DEPTH_2 = 2

GRID_W = 64
CTX_LEN = 256
N_MIXERS = 3
ROPE_BASE = 10000.0
Q_BLOCK = 128
N_MOD = 6

MLA_HEADS = 8
MLA_NOPE = 128
MLA_ROPE = 64
MLA_V = 128
MLA_Q_RANK = 384
MLA_KV_RANK = 256

HG_HEADS = 8
HG_DK = D_MODEL // HG_HEADS
HG_DV = D_MODEL // HG_HEADS
HG_CHUNK = 64

DF_HEADS = 8
DF_DQK = D_MODEL // (2 * DF_HEADS)
DF_DV = 2 * DF_DQK

D_FF = -(-(8 * D_MODEL) // (3 * 256)) * 256

N_MLA = (DEPTH_2 + N_MIXERS - 1) // N_MIXERS
N_HG = (DEPTH_2 + N_MIXERS - 2) // N_MIXERS
N_DF = DEPTH_2 // N_MIXERS


def rms_norm(x, w):
    xf = x.astype(jnp.float32)
    y = xf * lax.rsqrt(jnp.mean(xf * xf, axis=-1, keepdims=True) + EPS)
    return (y * w.astype(jnp.float32)).astype(x.dtype)

def modulate(x, shift, scale):
    return x * (1 + scale) + shift

def swiglu(a, w1, w3, w2):
    return (jax.nn.silu(a @ w1) * (a @ w3)) @ w2

def split_heads(t, n_heads):
    b, n, _ = t.shape
    return t.reshape(b, n, n_heads, -1).transpose(0, 2, 1, 3)

def merge_heads(t):
    b, h, n, d = t.shape
    return t.transpose(0, 2, 1, 3).reshape(b, n, h * d)

def axial_rope_tables(rows, rot_dim):
    row = jnp.repeat(jnp.arange(rows, dtype=jnp.float32), GRID_W)
    col = jnp.tile(jnp.arange(GRID_W, dtype=jnp.float32), rows)
    axis_dim = rot_dim // 2
    inv_freq = jnp.power(ROPE_BASE, -jnp.arange(0, axis_dim, 2, dtype=jnp.float32) / axis_dim)
    ang_r = row[:, None] * inv_freq
    ang_c = col[:, None] * inv_freq
    ang = jnp.concatenate([ang_r, ang_r, ang_c, ang_c], axis=-1)
    return jnp.cos(ang), jnp.sin(ang)

def apply_axial_rope(t, cos, sin):
    t1, t2, t3, t4 = jnp.split(t, 4, axis=-1)
    rot = jnp.concatenate([-t2, t1, -t4, t3], axis=-1)
    return (t * cos + rot * sin).astype(t.dtype)

def softmax_attend(q, k, v, scale):
    s = jnp.einsum('bhqd,bhkd->bhqk', q, k, preferred_element_type=jnp.float32) * scale
    p = jax.nn.softmax(s, axis=-1)
    return jnp.einsum('bhqk,bhkd->bhqd', p.astype(v.dtype), v)

def sweep_query_blocks(fn, q):
    n, d = q.shape[-2], q.shape[-1]
    nb = n // Q_BLOCK
    qb = jnp.moveaxis(q.reshape(q.shape[:-2] + (nb, Q_BLOCK, d)), -3, 0)
    o = jnp.moveaxis(lax.map(fn, qb), 0, -3)
    return o.reshape(o.shape[:-3] + (n, o.shape[-1]))

def gla_chunk_scan(q, k, v, log_f, s0):
    b, h, n, _ = q.shape
    nc = n // HG_CHUNK

    def chunks(t):
        return jnp.moveaxis(t.reshape(b, h, nc, HG_CHUNK, t.shape[-1]), 2, 0)

    order = jnp.tril(jnp.ones((HG_CHUNK, HG_CHUNK), dtype=bool))[:, :, None]

    def step(state, inp):
        qc, kc, vc, lfc = inp
        cum = jnp.cumsum(lfc, axis=-2)
        rel = jnp.where(order, cum[..., :, None, :] - cum[..., None, :, :], -jnp.inf)
        att = jnp.einsum('bhtd,bhsd,bhtsd->bhts', qc, kc, jnp.exp(rel))
        o = (jnp.einsum('bhts,bhse->bhte', att, vc)
             + jnp.einsum('bhtd,bhde->bhte', qc * jnp.exp(cum), state))
        last = cum[..., -1:, :]
        state = (jnp.exp(last[..., 0, :])[..., None] * state
                 + jnp.einsum('bhsd,bhse->bhde', kc * jnp.exp(last - cum), vc))
        return state, o

    state, o = lax.scan(step, s0, (chunks(q), chunks(k), chunks(v), chunks(log_f)))
    o = jnp.moveaxis(o, 0, 2).reshape(b, h, n, v.shape[-1])
    return o, state

def mla_mixer(a_lat, a_ctx, rope, w_in, q_norm_w, kv_norm_w, w_uq, w_ukv, qn_w, qr_w, kn_w, kr_w, w_o, update_ctx):
    cos, sin = rope

    def project(a):
        b, n, _ = a.shape
        cq, ckv, kr = jnp.split(a @ w_in, [MLA_Q_RANK, MLA_Q_RANK + MLA_KV_RANK], axis=-1)
        q = split_heads(rms_norm(cq, q_norm_w) @ w_uq, MLA_HEADS)
        kv = split_heads(rms_norm(ckv, kv_norm_w) @ w_ukv, MLA_HEADS)
        q_nope = rms_norm(q[..., :MLA_NOPE], qn_w)
        q_rope = rms_norm(q[..., MLA_NOPE:], qr_w)
        k_nope = rms_norm(kv[..., :MLA_NOPE], kn_w)
        v = kv[..., MLA_NOPE:]
        k_rope = rms_norm(kr, kr_w)[:, None]
        return q_nope, q_rope, k_nope, k_rope, v

    def full_k(kn, kr):
        return jnp.concatenate([kn, jnp.broadcast_to(kr, kn.shape[:-1] + (MLA_ROPE,))], axis=-1)

    qn_l, qr_l, kn_l, kr_l, v_l = project(a_lat)
    qr_l = apply_axial_rope(qr_l, cos, sin)
    kr_l = apply_axial_rope(kr_l, cos, sin)
    qn_c, qr_c, kn_c, kr_c, v_c = project(a_ctx)
    k_c = full_k(kn_c, kr_c)
    k_all = jnp.concatenate([k_c, full_k(kn_l, kr_l)], axis=-2)
    v_all = jnp.concatenate([v_c, v_l], axis=-2)
    scale = 1.0 / math.sqrt(MLA_NOPE + MLA_ROPE)
    q_l = jnp.concatenate([qn_l, qr_l], axis=-1)
    o_l = sweep_query_blocks(lambda qb: softmax_attend(qb, k_all, v_all, scale), q_l)
    out_l = merge_heads(o_l) @ w_o
    out_c = None
    if update_ctx:
        q_c = jnp.concatenate([qn_c, qr_c], axis=-1)
        out_c = merge_heads(softmax_attend(q_c, k_c, v_c, scale)) @ w_o
    return out_l, out_c

def hgrn2_mixer(a_lat, a_ctx, layer_idx, w_in, lb_logits, o_norm_w, w_o, update_ctx):
    lb_cum = jnp.cumsum(jax.nn.softmax(lb_logits.astype(jnp.float32), axis=0), axis=0)
    lb = lb_cum[layer_idx] - lb_cum[0]

    def project(a):
        q, zf, zb, i, g = jnp.split(a @ w_in, 5, axis=-1)

        def heads(t):
            return split_heads(t, HG_HEADS).astype(jnp.float32)

        def log_forget(z, lbd):
            lbd = lbd.reshape(HG_HEADS, 1, HG_DK)
            return jnp.logaddexp(jnp.log(lbd), jnp.log1p(-lbd) + jax.nn.log_sigmoid(heads(z)))

        return heads(q), heads(i), log_forget(zf, lb[0]), log_forget(zb, lb[1]), g

    def scan_dir(q, i, log_f, s0):
        return gla_chunk_scan(q, -jnp.expm1(log_f), i, log_f, s0)

    def rev(t):
        return jnp.flip(t, axis=-2)

    def readout(o, g):
        o = rms_norm(o.astype(a_lat.dtype), o_norm_w)
        return (merge_heads(o) * jax.nn.silu(g)) @ w_o

    q_l, i_l, lf_l, lbk_l, g_l = project(a_lat)
    q_c, i_c, lf_c, lbk_c, g_c = project(a_ctx)
    s0 = jnp.zeros((a_ctx.shape[0], HG_HEADS, HG_DK, HG_DV), jnp.float32)
    o_cf, s_cf = scan_dir(q_c, i_c, lf_c, s0)
    o_cb, s_cb = scan_dir(rev(q_c), rev(i_c), rev(lbk_c), s0)
    o_lf, _ = scan_dir(q_l, i_l, lf_l, s_cf)
    o_lb, _ = scan_dir(rev(q_l), rev(i_l), rev(lbk_l), s_cb)
    out_l = readout(o_lf + rev(o_lb), g_l)
    out_c = readout(o_cf + rev(o_cb), g_c) if update_ctx else None
    return out_l, out_c

def diff_mixer(a_lat, a_ctx, rope, layer_idx, w_qkv, qn_w, kn_w, lam_vec, sub_norm_w, w_o, update_ctx):
    cos, sin = rope
    lam_init = 0.8 - 0.6 * math.exp(-0.3 * layer_idx)
    lv = lam_vec.astype(jnp.float32)
    lam = jnp.exp(jnp.sum(lv[0] * lv[1])) - jnp.exp(jnp.sum(lv[2] * lv[3])) + lam_init

    def project(a):
        b, n, _ = a.shape
        q, k, v = jnp.split(a @ w_qkv, 3, axis=-1)
        q = rms_norm(q.reshape(b, n, DF_HEADS, 2, DF_DQK).transpose(0, 2, 3, 1, 4), qn_w)
        k = rms_norm(k.reshape(b, n, DF_HEADS, 2, DF_DQK).transpose(0, 2, 3, 1, 4), kn_w)
        return q, k, split_heads(v, DF_HEADS)

    scale = 1.0 / math.sqrt(DF_DQK)

    def diff_attend(q, k, v):
        s = jnp.einsum('bhmqd,bhmkd->bhmqk', q, k, preferred_element_type=jnp.float32) * scale
        p = jax.nn.softmax(s, axis=-1)
        a = p[:, :, 0] - lam * p[:, :, 1]
        return jnp.einsum('bhqk,bhkd->bhqd', a.astype(v.dtype), v)

    def readout(o):
        return merge_heads(rms_norm(o, sub_norm_w) * (1.0 - lam_init)) @ w_o

    q_l, k_l, v_l = project(a_lat)
    q_l = apply_axial_rope(q_l, cos, sin)
    k_l = apply_axial_rope(k_l, cos, sin)
    q_c, k_c, v_c = project(a_ctx)
    k_all = jnp.concatenate([k_c, k_l], axis=-2)
    v_all = jnp.concatenate([v_c, v_l], axis=-2)
    out_l = readout(sweep_query_blocks(lambda qb: diff_attend(qb, k_all, v_all), q_l))
    out_c = readout(diff_attend(q_c, k_c, v_c)) if update_ctx else None
    return out_l, out_c

def second_inputs(seed: int = 0) -> dict:
    key = jax.random.key(seed)
    ks = iter(jax.random.split(key, 40))
    D = D_MODEL

    def nrm(shape, scale):
        return scale * jax.random.normal(next(ks), shape, jnp.float32)

    def gain(shape):
        return 1.0 + nrm(shape, 0.02)

    return {
        'x': nrm((BATCH, SEQ, D), 1.0),
        'c': nrm((BATCH, D), 1.0),
        'ctx': nrm((BATCH, CTX_LEN, D), 1.0),
        'c_ctx': nrm((D,), 1.0),
        'ada_w': nrm((DEPTH_2, D, N_MOD * D), 0.5 * D ** -0.5),
        'ada_b': nrm((DEPTH_2, N_MOD * D), 0.02),
        'norm1_w': gain((DEPTH_2, D)),
        'norm2_w': gain((DEPTH_2, D)),
        'ffn_w1': nrm((DEPTH_2, D, D_FF), D ** -0.5),
        'ffn_w3': nrm((DEPTH_2, D, D_FF), D ** -0.5),
        'ffn_w2': nrm((DEPTH_2, D_FF, D), D_FF ** -0.5),
        'mla_w_in': nrm((N_MLA, D, MLA_Q_RANK + MLA_KV_RANK + MLA_ROPE), D ** -0.5),
        'mla_q_norm_w': gain((N_MLA, MLA_Q_RANK)),
        'mla_kv_norm_w': gain((N_MLA, MLA_KV_RANK)),
        'mla_w_uq': nrm((N_MLA, MLA_Q_RANK, MLA_HEADS * (MLA_NOPE + MLA_ROPE)), MLA_Q_RANK ** -0.5),
        'mla_w_ukv': nrm((N_MLA, MLA_KV_RANK, MLA_HEADS * (MLA_NOPE + MLA_V)), MLA_KV_RANK ** -0.5),
        'mla_qn_w': gain((N_MLA, MLA_NOPE)),
        'mla_qr_w': gain((N_MLA, MLA_ROPE)),
        'mla_kn_w': gain((N_MLA, MLA_NOPE)),
        'mla_kr_w': gain((N_MLA, MLA_ROPE)),
        'mla_w_o': nrm((N_MLA, MLA_HEADS * MLA_V, D), (MLA_HEADS * MLA_V) ** -0.5),
        'hg_w_in': nrm((N_HG, D, 5 * D), D ** -0.5),
        'hg_lb_logits': nrm((DEPTH_2, 2, D), 1.0),
        'hg_o_norm_w': gain((N_HG, HG_DV)),
        'hg_w_o': nrm((N_HG, D, D), D ** -0.5),
        'df_w_qkv': nrm((N_DF, D, 3 * D), D ** -0.5),
        'df_qn_w': gain((N_DF, DF_DQK)),
        'df_kn_w': gain((N_DF, DF_DQK)),
        'df_lambda': nrm((N_DF, 4, DF_DQK), 0.1),
        'df_sub_norm_w': gain((N_DF, DF_DV)),
        'df_w_o': nrm((N_DF, D, D), D ** -0.5),
    }

def second_block(x, c, ctx, c_ctx, ada_w, ada_b, norm1_w, norm2_w, ffn_w1, ffn_w3, ffn_w2,
              mla_w_in, mla_q_norm_w, mla_kv_norm_w, mla_w_uq, mla_w_ukv, mla_qn_w, mla_qr_w, mla_kn_w,
              mla_kr_w, mla_w_o, hg_w_in, hg_lb_logits, hg_o_norm_w, hg_w_o,
              df_w_qkv, df_qn_w, df_kn_w, df_lambda, df_sub_norm_w, df_w_o):
    rows = x.shape[1] // GRID_W
    rope_mla = axial_rope_tables(rows, MLA_ROPE)
    rope_df = axial_rope_tables(rows, DF_DQK)
    h_ctx = ctx
    for i in range(DEPTH_2):
        kind, j = i % N_MIXERS, i // N_MIXERS
        update_ctx = i < DEPTH_2 - 1
        mod_l = jnp.split((jax.nn.silu(c) @ ada_w[i] + ada_b[i])[:, None, :], N_MOD, axis=-1)
        mod_c = jnp.split((jax.nn.silu(c_ctx) @ ada_w[i] + ada_b[i])[None, None, :], N_MOD, axis=-1)
        a_l = modulate(rms_norm(x, norm1_w[i]), mod_l[0], mod_l[1])
        a_c = modulate(rms_norm(h_ctx, norm1_w[i]), mod_c[0], mod_c[1])
        if kind == 0:
            o_l, o_c = mla_mixer(a_l, a_c, rope_mla, mla_w_in[j], mla_q_norm_w[j], mla_kv_norm_w[j],
                                 mla_w_uq[j], mla_w_ukv[j], mla_qn_w[j], mla_qr_w[j], mla_kn_w[j],
                                 mla_kr_w[j], mla_w_o[j], update_ctx)
        elif kind == 1:
            o_l, o_c = hgrn2_mixer(a_l, a_c, i, hg_w_in[j], hg_lb_logits, hg_o_norm_w[j], hg_w_o[j], update_ctx)
        else:
            o_l, o_c = diff_mixer(a_l, a_c, rope_df, i, df_w_qkv[j], df_qn_w[j], df_kn_w[j], df_lambda[j],
                                  df_sub_norm_w[j], df_w_o[j], update_ctx)
        x = x + mod_l[2] * o_l
        x = x + mod_l[5] * swiglu(modulate(rms_norm(x, norm2_w[i]), mod_l[3], mod_l[4]),
                                  ffn_w1[i], ffn_w3[i], ffn_w2[i])
        if update_ctx:
            h_ctx = h_ctx + mod_c[2] * o_c
            h_ctx = h_ctx + mod_c[5] * swiglu(modulate(rms_norm(h_ctx, norm2_w[i]), mod_c[3], mod_c[4]),
                                              ffn_w1[i], ffn_w3[i], ffn_w2[i])
    return x


def setup_inputs(seed=0):
    out = dict(first_inputs(seed))
    for name, value in second_inputs(seed + 1).items():
        if name != "x":
            out[name + "_2"] = value
    return out


def reference(
    x, p, attn_norm, w_in, kv_norm, w_uk, w_uv, rel_bias, w_branch_a, w_branch_b, w_out,
    ffn_norm, w_r1, b_r1, w_r2, b_r2, w_gate, w_up, w_down, ple_norm, w_ple_gate, w_ple,
    final_norm, c_2, ctx_2, c_ctx_2, ada_w_2, ada_b_2, norm1_w_2, norm2_w_2, ffn_w1_2, ffn_w3_2,
    ffn_w2_2, mla_w_in_2, mla_q_norm_w_2, mla_kv_norm_w_2, mla_w_uq_2, mla_w_ukv_2, mla_qn_w_2,
    mla_qr_w_2, mla_kn_w_2, mla_kr_w_2, mla_w_o_2, hg_w_in_2, hg_lb_logits_2, hg_o_norm_w_2,
    hg_w_o_2, df_w_qkv_2, df_qn_w_2, df_kn_w_2, df_lambda_2, df_sub_norm_w_2, df_w_o_2,
):
    x = first_block(
        x, p, attn_norm, w_in, kv_norm, w_uk, w_uv, rel_bias, w_branch_a, w_branch_b, w_out,
        ffn_norm, w_r1, b_r1, w_r2, b_r2, w_gate, w_up, w_down, ple_norm, w_ple_gate, w_ple,
        final_norm,
    )
    return second_block(
        x, c_2, ctx_2, c_ctx_2, ada_w_2, ada_b_2, norm1_w_2, norm2_w_2, ffn_w1_2, ffn_w3_2,
        ffn_w2_2, mla_w_in_2, mla_q_norm_w_2, mla_kv_norm_w_2, mla_w_uq_2, mla_w_ukv_2,
        mla_qn_w_2, mla_qr_w_2, mla_kn_w_2, mla_kr_w_2, mla_w_o_2, hg_w_in_2, hg_lb_logits_2,
        hg_o_norm_w_2, hg_w_o_2, df_w_qkv_2, df_qn_w_2, df_kn_w_2, df_lambda_2, df_sub_norm_w_2,
        df_w_o_2,
    )


_drawn_inputs = setup_inputs


def setup_inputs(seed=0):
    import zlib

    import numpy as np

    out = dict(_drawn_inputs(seed))
    spreads = {}
    factors = {'kv_norm': 2.857,
     'b_r1': 8.0,
     'b_r2': 6.365,
     'ple_norm': 5.958,
     'ctx_2': 3.842,
     'norm1_w_2': 6.856,
     'norm2_w_2': 6.493,
     'mla_q_norm_w_2': 8.0,
     'mla_kv_norm_w_2': 8.0,
     'mla_qn_w_2': 8.0,
     'mla_qr_w_2': 8.0,
     'mla_kn_w_2': 8.0,
     'mla_kr_w_2': 8.0,
     'hg_o_norm_w_2': 8.0}
    for name, (base, spread) in spreads.items():
        noise = np.random.default_rng([zlib.crc32(name.encode()), seed]).standard_normal(out[name].shape)
        drawn = base * np.exp(spread * noise) if base else spread * noise
        out[name] = jnp.asarray(drawn.astype(out[name].dtype))
    for name, factor in factors.items():
        out[name] = (out[name] * factor).astype(out[name].dtype)
    return out
```

```python
from contextlib import ExitStack

import numpy as np

import concourse.bass as bass
from concourse import mybir

F32 = mybir.dt.float32
U32 = mybir.dt.uint32
ALU = mybir.AluOpType
ACT = mybir.ActivationFunctionType
AX = mybir.AxisListType.X
ds = bass.ds

P = 128
D = 1024
KD = D // P
T = 512
C = 256
N = T + C
QT = T // P
EPS = 1e-6
HEADS = 8
HD = 64
TOPK = 128
NEG = -1e30
TAKEN = -3e38
N_EXP = 32
D_FF = 2816
KF = D_FF // P
RING = 4
SLOT = KF * P
BANK = 512


def each_round(eng, panels, body):
    full, rest = divmod(panels, RING)
    if full > 1:
        with eng.Fori(0, full) as i:
            body(i, RING)
    elif full == 1:
        body(0, RING)
    if rest:
        body(full, rest)


class Chip:

    def __init__(self, nc, ctx, dram):
        self.nc, self.ctx, self.dram, self.own = nc, ctx, dram, []
        self.ring = self.sb("ring", [P, RING, SLOT])
        self.flat = self.ring[:, :, :].rearrange("p a b -> p (a b)")
        self.x = self.sb("residual", [P, KD, N])
        self.h = self.sb("normed", [P, KD, N])
        self.ones = self.sb("ones", [P, P])
        self.ident = self.sb("ident", [P, P])
        self.eps = self.sb("eps", [P, 1])
        self.vec = self.sb("vectors", [P, VEC_COLS])
        self.mod = self.sb("modulation", [P, 2, 48, 2])
        self.gain = self.sb("gains", [P, 2, 2, KD, 2])
        self.ps = ctx.enter_context(nc.psum_tensor("ps", [P, 8, BANK], F32))
        self.psf = self.ps[:, :, :].rearrange("p b n -> p (b n)")

    def sb(self, name, shape, dt=F32):
        return self.ctx.enter_context(self.nc.sbuf_tensor(name, shape, dt))

    def sem(self, name):
        s = self.nc.alloc_semaphore(name)
        self.own.append(s)
        return s

    def end(self):
        for s in self.own:
            self.nc.gpsimd.sem_clear(s)
            self.nc.release_semaphore(s)
        self.own = []

    def v(self, name, k=0, rows=P):
        at = VEC_AT[name][0] + k
        return self.vec[0:rows, at:at + 1]


VECS = [("attn_norm", KD), ("ffn_norm", KD), ("ple_norm", KD), ("final_norm", KD), ("kv_norm", 1),
        ("norm1_0", KD), ("norm1_1", KD), ("norm2_0", KD), ("norm2_1", KD),
        ("q_norm", 3), ("mkv_norm", 2), ("qn", 1), ("qr", 1), ("kn", 1), ("kr", 1),
        ("o_norm", 1), ("b_ada_0", 48), ("b_ada_1", 48), ("lb0_f", KD), ("lb0_b", KD),
        ("lb1_f", KD), ("lb1_b", KD), ("c_lat", KD), ("c_ctx", KD)]
VEC_AT = {}
VEC_COLS = 0
for _name, _n in VECS:
    VEC_AT[_name] = (VEC_COLS, _n)
    VEC_COLS += _n


def linear(K, name, w, panels, banks, groups, words, on_act=None, on_dve=None, first=0):
    nc = K.nc
    turns = min(RING, 8 // banks)
    loaded = [K.sem(f"{name}_loaded{j}") for j in range(RING)]
    product = [K.sem(f"{name}_product{j}") for j in range(RING)]
    act_done = [K.sem(f"{name}_act{j}") for j in range(RING)] if on_act else None
    dve_done = [K.sem(f"{name}_dve{j}") for j in range(RING)] if on_dve else None

    def set_of(j):
        t = j % turns
        return [K.ps[:, b, :] for b in range(t * banks, (t + 1) * banks)]

    with nc.Block() as block:
        @block.sync
        def _(sp):
            def body(i, n):
                for j in range(n):
                    sp.wait_ge(product[j], i + 1)
                    sp.dma_start(K.ring[:, j, 0:words], w[first + i * RING + j]).then_inc(loaded[j], 16)
            each_round(sp, panels, body)

        @block.tensor
        def _(pe):
            def body(i, n):
                for j in range(n):
                    for done in (act_done, dve_done):
                        if done and j < turns:
                            pe.wait_ge(done[max(s for s in range(RING) if s % turns == j)], i + 1)
                        elif done:
                            pe.wait_ge(done[j - turns], i + 2)
                    pe.wait_ge(loaded[j], (i + 1) * 16)
                    for b, at, cols, rows, terms in groups(j):
                        for t, (lhs, rhs) in enumerate(terms):
                            mm = pe.matmul(set_of(j)[b][0:rows, at:at + cols], lhs, rhs,
                                           start=t == 0, stop=t == len(terms) - 1)
                    mm.then_inc(product[j], 1)
            for j in range(RING):
                pe.sem_inc(product[j], 1)
            each_round(pe, panels, body)

        if on_act:
            @block.scalar
            def _(act):
                def body(i, n):
                    for j in range(n):
                        act.wait_ge(product[j], i + 2)
                        on_act(act, i * RING + j, set_of(j)).then_inc(act_done[j], 1)
                for j in range(RING):
                    act.sem_inc(act_done[j], 1)
                each_round(act, panels, body)

        if on_dve:
            @block.vector
            def _(dve):
                def body(i, n):
                    for j in range(n):
                        dve.wait_ge(product[j], i + 2)
                        if act_done:
                            dve.wait_ge(act_done[j], i + 2)
                        on_dve(dve, i * RING + j, set_of(j)).then_inc(dve_done[j], 1)
                for j in range(RING):
                    dve.sem_inc(dve_done[j], 1)
                each_round(dve, panels, body)
    K.end()


def features_out(K, acts, kc, width, spans):
    def groups(j):
        out = []
        for w in range(width // P):
            for s, (a, c) in enumerate(spans):
                out.append((w * len(spans) + s, 0, c, P,
                            [(K.ring[:, j, k * width + w * P:k * width + (w + 1) * P], acts[:, k, a:a + c])
                             for k in range(kc)]))
        return out
    return groups


def load(K, name, pairs):
    with K.nc.Block() as block:
        here = K.sem(f"{name}_here")

        @block.sync
        def _(sp):
            for dst, src in pairs:
                sp.dma_start(dst, src).then_inc(here, 16)
            sp.wait_ge(here, 16 * len(pairs))
    K.end()


def rms(K, name, items, width, gain, shift=None, rows=P):
    nc = K.nc
    squared, summed = K.sem(f"{name}_squared"), K.sem(f"{name}_summed")
    rooted, scaled = K.sem(f"{name}_rooted"), K.sem(f"{name}_scaled")
    inverted = K.sem(f"{name}_inverted")
    with ExitStack() as own:
        sqs, root, inv = (K.flat[:, n * 2 * BANK:(n + 1) * 2 * BANK].rearrange("p (u n) -> p u n", u=2)
                          for n in range(3))
        steps = [(i, k) for i, (src, _, _) in enumerate(items) for k in range(len(src))]
        upto = [0]
        for src, _, _ in items:
            upto.append(upto[-1] + len(src))
        block = own.enter_context(nc.Block())

        @block.scalar
        def _(act):
            def root_of(i):
                c = items[i][2]
                act.wait_ge(summed, upto[i + 1])
                if i >= 2:
                    act.wait_ge(inverted, i - 1)
                act.activation(root[0:rows, i % 2, 0:c], K.ps[0:rows, i % 4, 0:c], ACT.Sqrt,
                               scale=1.0 / width, bias=K.eps[0:rows, :]).then_inc(rooted, 1)
            for n, (i, k) in enumerate(steps):
                if k == 0 and i > 0:
                    root_of(i - 1)
                if n >= 2:
                    act.wait_ge(summed, n - 1)
                act.activation(sqs[0:rows, n % 2, 0:items[i][2]], items[i][0][k], ACT.Square).then_inc(squared, 1)
            root_of(len(items) - 1)
            if shift:
                for n, (i, k) in enumerate(steps):
                    act.wait_ge(scaled, n + 1)
                    act.activation(items[i][1][k], items[i][1][k], ACT.Identity, bias=shift(i, k))

        @block.tensor
        def _(pe):
            for n, (i, k) in enumerate(steps):
                c = items[i][2]
                if k == 0 and i >= 4:
                    pe.wait_ge(rooted, i - 3)
                pe.wait_ge(squared, n + 1)
                pe.matmul(K.ps[0:rows, i % 4, 0:c], K.ones[0:rows, 0:rows], sqs[0:rows, n % 2, 0:c],
                          start=k == 0, stop=n + 1 == upto[i + 1]).then_inc(summed, 1)

        @block.vector
        def _(dve):
            for i, (src, dst, c) in enumerate(items):
                dve.wait_ge(rooted, i + 1)
                if i >= 2:
                    dve.wait_ge(scaled, upto[i - 1])
                dve.reciprocal(inv[0:rows, i % 2, 0:c], root[0:rows, i % 2, 0:c]).then_inc(inverted, 1)
                dve.wait_ge(inverted, i + 1)
                for k in range(len(src)):
                    dve.scalar_tensor_tensor(out=dst[k], in0=src[k], scalar=gain(i, k), in1=inv[0:rows, i % 2, 0:c],
                                             op0=ALU.mult, op1=ALU.mult).then_inc(scaled, 1)
    K.end()


def norm_model(K, name, spans, gain, shift=None):
    items = [([K.x[:, k, a:a + c] for k in range(KD)], [K.h[:, k, a:a + c] for k in range(KD)], c)
             for a, c in spans]
    rms(K, name, items, D, gain, shift)


LAT = [(0, T)]
BOTH = [(0, T), (T, C)]

QA, CKV, KIDX, QIDX, QB, KB, GA, GB = 0, 4, 5, 6, 10, 14, 18, 26


def copy_pair(dst, base=0):
    def take(dve, m, banks):
        dve.tensor_copy(dst[:, m * 2 + base, :], banks[0])
        return dve.tensor_copy(dst[:, m * 2 + base + 1, :], banks[1])
    return take


def project_in(K, proj, vb, widx):
    groups = features_out(K, K.h, KD, 256, LAT)
    linear(K, "w_in", K.dram["w_main"], 9, 2, groups, 2048, on_dve=copy_pair(proj))

    def sigmoids(act, m, banks):
        act.activation(proj[:, m * 2 + GA, :], banks[0], ACT.Sigmoid)
        return act.activation(proj[:, m * 2 + GA + 1, :], banks[1], ACT.Sigmoid)
    linear(K, "w_gates", K.dram["w_main"], 8, 2, groups, 2048, on_act=sigmoids, first=9)

    def tokens_out(j):
        return [(0 if q < 2 else 1, (q % 2) * 256, 256, P,
                 [(K.h[:, k, q * P:(q + 1) * P], K.ring[:, j, k * 256:(k + 1) * 256]) for k in range(KD)])
                for q in range(QT)]

    def take_v(dve, m, banks):
        for q in range(QT):
            last = dve.tensor_copy(vb[:, q, ds(m * 256, 256)], banks[q // 2][:, (q % 2) * 256:(q % 2 + 1) * 256])
        return last
    linear(K, "w_vb", K.dram["w_vb"], 2, 2, tokens_out, 2048, on_dve=take_v)

    def idx_out(j):
        return [(0, q * 8, 8, P, [(K.h[:, k, q * P:(q + 1) * P], K.ring[:, j, k * 8:(k + 1) * 8])
                                  for k in range(KD)]) for q in range(QT)]

    def take_w(dve, m, banks):
        return dve.tensor_scalar(widx[:, :], banks[0][:, 0:QT * 8], (HEADS ** -0.5) * (HD ** -0.5), None, ALU.mult)
    linear(K, "w_idx", K.dram["w_idx"], 1, 2, idx_out, 64, on_dve=take_w)


def bias_tiles(K):
    nc, d = K.nc, K.dram
    made, taken, stored, back, here = (K.sem(f"bias_{n}") for n in ("made", "taken", "stored", "back", "here"))
    with ExitStack() as own:
        rel = own.enter_context(nc.sbuf_tensor("rel", [32, HEADS], F32))
        wide = own.enter_context(nc.sbuf_tensor("rel_wide", [32, HEADS, P], F32))
        hot = own.enter_context(nc.sbuf_tensor("bucket_hot", [32, SKEW], F32))
        rows = K.flat[:, 0:HEADS * SKEW].rearrange("p (h n) -> p h n", h=HEADS)
        spread = K.sem("bias_spread")
        block = own.enter_context(nc.Block())

        @block.sync
        def _(sp):
            sp.dma_start(rel[:, :], d["rel_bias"]).then_inc(here, 16)
            sp.dma_start(hot[:, :], d["buckets"]).then_inc(here, 16)
            sp.wait_ge(taken, 2 * HEADS)
            sp.dma_start(d["skew"][:, :, 0:SKEW].rearrange("h p n -> p h n"), rows).then_inc(stored, 16)
            sp.wait_ge(stored, 16)
            skewed = d["skew_flat"][:, 0:P * SKEW].rearrange("h (p n) -> p h n", p=P)
            sp.dma_start(K.bias, skewed[:, :, P - 1:P - 1 + T]).then_inc(back, 16)
            sp.wait_ge(back, 16)

        @block.vector
        def _(dve):
            dve.wait_ge(here, 32)
            dve.tensor_copy(wide[:, :, :], rel[:, :].unsqueeze(2).to_broadcast([32, HEADS, P])).then_inc(spread, 1)
            for n in range(2 * HEADS):
                h, half = divmod(n, 2)
                dve.wait_ge(made, n + 1)
                dve.tensor_copy(rows[:, h, half * SKEW // 2:(half + 1) * SKEW // 2],
                                K.ps[:, n % 4, 0:SKEW // 2]).then_inc(taken, 1)

        @block.tensor
        def _(pe):
            pe.wait_ge(spread, 1)
            for n in range(2 * HEADS):
                h, half = divmod(n, 2)
                if n >= 4:
                    pe.wait_ge(taken, n - 3)
                pe.matmul(K.ps[:, n % 4, 0:SKEW // 2], wide[:, h, :], hot[:, half * SKEW // 2:(half + 1) * SKEW // 2],
                          start=True, stop=True).then_inc(made, 1)
    K.end()


SKEW = 640


def half(h):
    return (h % 2) * HD, (h % 2 + 1) * HD


def select_keys(K, proj, widx, maskadd, cneg):
    nc = K.nc
    scored, positive, summed, chain = (K.sem(f"sel_{n}") for n in ("scored", "positive", "summed", "chain"))
    rel = K.flat[:, 0:2 * T].rearrange("p (b n) -> p b n", b=2)
    score = K.flat[:, 2 * T:4 * T].rearrange("p (b n) -> p b n", b=2)
    top = K.flat[:, 4 * T:4 * T + 8]
    tasks = [(i, h) for i in range(1, QT) for h in range(HEADS)]
    with nc.Block() as block:
        @block.tensor
        def _(pe):
            for n, (i, h) in enumerate(tasks):
                a, b = half(h)
                if n >= 4:
                    pe.wait_ge(positive, n - 3)
                pe.matmul(K.ps[:, n % 4, 0:(i + 1) * P], proj[a:b, QIDX + h // 2, i * P:(i + 1) * P],
                          proj[a:b, KIDX, 0:(i + 1) * P], start=True, stop=True).then_inc(scored, 1)

        @block.scalar
        def _(act):
            for n, (i, h) in enumerate(tasks):
                act.wait_ge(scored, n + 1)
                if n >= 2:
                    act.wait_ge(summed, n - 1)
                act.activation(rel[:, n % 2, 0:(i + 1) * P], K.ps[:, n % 4, 0:(i + 1) * P],
                               ACT.Relu).then_inc(positive, 1)

        @block.vector
        def _(dve):
            steps = [0]

            def link(ins):
                steps[0] += 1
                ins.then_inc(chain, 1)
                dve.wait_ge(chain, steps[0])

            dve.tensor_copy(maskadd[:, 0, 0:P], cneg)
            for n, (i, h) in enumerate(tasks):
                w = (i + 1) * P
                s = score[:, i % 2, 0:w]
                dve.wait_ge(positive, n + 1)
                if h == 0:
                    dve.tensor_scalar(s, rel[:, n % 2, 0:w], widx[:, i * 8 + h:i * 8 + h + 1], None,
                                      ALU.mult).then_inc(summed, 1)
                else:
                    dve.scalar_tensor_tensor(out=s, in0=rel[:, n % 2, 0:w], scalar=widx[:, i * 8 + h:i * 8 + h + 1],
                                             in1=s, op0=ALU.mult, op1=ALU.add).then_inc(summed, 1)
                dve.wait_ge(summed, n + 1)
                if h == HEADS - 1:
                    diag = score[:, i % 2, i * P:w]
                    link(dve.tensor_tensor(diag, diag, cneg, ALU.add))
                    for _ in range(TOPK // 8):
                        link(dve.max(top, s))
                        link(dve.match_replace(s, top, s, TAKEN))
                    dve.tensor_scalar(maskadd[:, i, 0:w], s, TAKEN / 2, NEG, ALU.is_gt, ALU.mult)
    K.end()


def attend(K, name, tasks, spare, heads, scale, values, out, bias=False):
    nc = K.nc
    names = ("scored", "shown", "maxed", "exped", "normed", "turned", "copied", "valued", "outed", "chain")
    scored, shown, maxed, exped, normed, turned, copied, valued, outed, chain = (
        K.sem(f"{name}_{n}") for n in names)
    blocks, queries, width = spare
    at = [0]

    def part(*shape):
        n = int(np.prod(shape))
        ap = K.flat[:, at[0]:at[0] + n]
        at[0] += n
        return ap

    turn = [part(blocks * queries).rearrange("p (k q) -> p k q", k=blocks) for _ in range(2)]
    prob = [part(width) for _ in range(2)]
    logit = [part(width) for _ in range(2)] if bias else None
    last = [t + 1 == len(tasks) or tasks[t + 1][0] != task[0] for t, task in enumerate(tasks)]
    outs = len(out(0))
    with ExitStack() as own:
        small = own.enter_context(nc.sbuf_tensor(f"{name}_small", [P, 4, 4], F32))
        block = own.enter_context(nc.Block())

        def raw(n):
            b = (n % 2) * 2 * BANK
            return K.psf[:, b:b + tasks[n][1]]

        @block.tensor
        def _(pe):
            def scores(n):
                _, w, terms, _, _, _, _ = tasks[n]
                if n >= 2:
                    pe.wait_ge(shown if bias else exped, n - 1)
                    pe.wait_ge(exped, n - 1)
                for c in range(0, w, BANK):
                    e = min(w, c + BANK)
                    for t, (q, k) in enumerate(terms):
                        mm = pe.matmul(raw(n)[:, c:e], q, k[:, c:e], start=t == 0, stop=t == len(terms) - 1)
                mm.then_inc(scored, 1)

            scores(0)
            for n, (h, w, _, _, _, _, _) in enumerate(tasks):
                if n + 1 < len(tasks):
                    scores(n + 1)
                pe.wait_ge(normed, n + 1)
                if n >= 1:
                    pe.wait_ge(copied, n)
                for b in range(w // P):
                    mm = pe.transpose(K.psf[:, 4 * BANK + b * P:4 * BANK + (b + 1) * P],
                                      prob[n % 2][:, b * P:(b + 1) * P], K.ident[:, :])
                mm.then_inc(turned, 1)
                if last[n]:
                    pe.wait_ge(copied, n + 1)
                    if h >= 1:
                        pe.wait_ge(outed, h)
                    for bank, a, e, terms in values(h, turn[h % 2]):
                        for t, (v, p, x) in enumerate(terms):
                            mm = pe.matmul(K.ps[:, bank, a + x:e], v, p, start=t == 0, stop=t == len(terms) - 1)
                    mm.then_inc(valued, 1)

        @block.vector
        def _(dve):
            links = [0]

            def link(ins):
                links[0] += 1
                ins.then_inc(chain, 1)
                dve.wait_ge(chain, links[0])

            def top(n):
                w = tasks[n][1]
                dve.wait_ge(scored, n + 1)
                if n >= 4:
                    dve.wait_ge(exped, n - 3)
                s = raw(n)
                if bias:
                    s = logit[n % 2][:, 0:w]
                    if n >= 2:
                        dve.wait_ge(exped, n - 1)
                    dve.scalar_tensor_tensor(out=s, in0=raw(n), scalar=scale, in1=tasks[n][5],
                                             op0=ALU.mult, op1=ALU.add).then_inc(shown, 1)
                    dve.wait_ge(shown, n + 1)
                    link(dve.tensor_tensor(s, s, tasks[n][6], ALU.add))
                link(dve.reduce_max(small[:, n % 4, 0:1], s, AX))
                dve.tensor_scalar(small[:, n % 4, 1:2], small[:, n % 4, 0:1], -1.0 if bias else -scale, None,
                                  ALU.mult).then_inc(maxed, 1)

            def outputs(dve, h):
                dve.wait_ge(valued, h + 1)
                for dst, bank, c in out(h):
                    ins = dve.tensor_copy(dst, K.ps[:, bank, 0:c])
                ins.then_inc(outed, 1)

            top(0)
            for n, (h, w, _, _, _, _, _) in enumerate(tasks):
                if n + 1 < len(tasks):
                    top(n + 1)
                dve.wait_ge(exped, n + 1)
                link(dve.reciprocal(small[:, n % 4, 3:4], small[:, n % 4, 2:3]))
                dve.tensor_scalar(prob[n % 2][:, 0:w], prob[n % 2][:, 0:w], small[:, n % 4, 3:4], None,
                                  ALU.mult).then_inc(normed, 1)
                if last[n] and h >= 1:
                    outputs(dve, h - 1)
            outputs(dve, heads - 1)

        @block.scalar
        def _(act):
            def exp(n):
                w = tasks[n][1]
                act.wait_ge(maxed, n + 1)
                if n >= 2:
                    act.wait_ge(turned, n - 1)
                act.activation(prob[n % 2][:, 0:w], logit[n % 2][:, 0:w] if bias else raw(n), ACT.Exp,
                               bias=small[:, n % 4, 1:2], scale=1.0 if bias else scale,
                               accum_out=small[:, n % 4, 2:3]).then_inc(exped, 1)

            exp(0)
            for n, (h, w, _, k0, q0, _, _) in enumerate(tasks):
                if n + 1 < len(tasks):
                    exp(n + 1)
                act.wait_ge(turned, n + 1)
                if h >= 2:
                    act.wait_ge(valued, h - 1)
                act.activation(turn[h % 2][:, k0:k0 + w // P, q0:q0 + P],
                               K.psf[:, 4 * BANK:4 * BANK + w].rearrange("p (k q) -> p k q", q=P),
                               ACT.Copy).then_inc(copied, 1)
    K.end()


def products(K, name, items):
    nc = K.nc
    made, taken = K.sem(f"{name}_made"), K.sem(f"{name}_taken")
    with nc.Block() as block:
        @block.tensor
        def _(pe):
            for n, ((a, b), cols, terms, _) in enumerate(items):
                if n >= 8:
                    pe.wait_ge(taken, n - 7)
                for t, (lhs, rhs) in enumerate(terms):
                    mm = pe.matmul(K.ps[a:b, n % 8, 0:cols], lhs, rhs, start=t == 0, stop=t == len(terms) - 1)
                mm.then_inc(made, 1)

        @block.vector
        def _(dve):
            for n, ((a, b), cols, _, dst) in enumerate(items):
                dve.wait_ge(made, n + 1)
                dve.tensor_copy(dst, K.ps[a:b, n % 8, 0:cols]).then_inc(taken, 1)
    K.end()


def sparse_attention(K, proj, widx, cneg):
    nc, d = K.nc, K.dram
    with ExitStack() as own:
        maskadd = own.enter_context(nc.sbuf_tensor("maskadd", [P, QT, T], F32))
        c_nat = own.enter_context(nc.sbuf_tensor("c_nat", [P, QT, P], F32))
        w_uk = own.enter_context(nc.sbuf_tensor("w_uk", [P, HEADS // 2, P], F32))
        w_uv = own.enter_context(nc.sbuf_tensor("w_uv", [P, HEADS, HD], F32))
        load(K, "load_uk", [(w_uk[:, :, :], d["w_uk"]), (w_uv[:, :, :], d["w_uv"])])
        rms(K, "kv_norm", [([proj[:, CKV, :]], [proj[:, CKV, :]], T)], P, lambda i, k: K.v("kv_norm"))
        select_keys(K, proj, widx, maskadd, cneg)
        bias_tiles(K)
        items = [((0, P), P, [(proj[:, CKV, q * P:(q + 1) * P], K.ident[:, :])], c_nat[:, q, :]) for q in range(QT)]
        q_abs = K.h
        for h in range(HEADS):
            a, b = half(h)
            items.append(((0, P), T, [(w_uk[a:b, h // 2, :], proj[a:b, QA + h // 2, :])], q_abs[:, h, 0:T]))
        products(K, "q_abs", items)

        def o_at(h):
            return proj[:, QA + h if h < 4 else QIDX + h - 4, :]

        tasks = []
        for h in range(HEADS):
            for i in range(QT):
                w = (i + 1) * P
                tasks.append((h, w, [(q_abs[:, h, i * P:w], proj[:, CKV, 0:w])], 0, i * P,
                              K.bias[:, h, T - w:T], maskadd[:, i, 0:w]))

        def values(h, turn):
            return [(6, 0, T, [(c_nat[:, b, :], turn[:, b, b * P:T], b * P) for b in range(QT)])]
        attend(K, "dsa", tasks, (QT, T, T), HEADS, HD ** -0.5, values, lambda h: [(o_at(h), 6, T)], bias=True)
        o_a = K.h
        products(K, "w_uv", [(half(h), T, [(w_uv[:, h, :], o_at(h))], o_a[half(h)[0]:half(h)[1], h // 2, 0:T])
                             for h in range(HEADS)])


def stick_breaking(K, proj, vb, sneg, s01, upper):
    nc = K.nc
    names = ("scored", "scaled", "folded", "faded", "softened", "masked", "summed", "logged", "weighed", "valued", "outed")
    scored, scaled, folded, faded, softened, masked, summed, logged, weighed, valued, outed = (
        K.sem(f"stick_{n}") for n in names)
    tasks = [(h, b) for h in range(HEADS) for b in reversed(range(QT))]
    z = K.flat[:, 0:2 * QT * T].rearrange("p (u b q) -> p u b q", u=2, b=QT)
    sp = K.flat[:, 2 * QT * T:4 * QT * T].rearrange("p (u b q) -> p u b q", u=2, b=QT)
    tmp = K.flat[:, 4 * QT * T:4 * QT * T + 4 * T].rearrange("p (u q) -> p u q", u=4)
    o_b = K.h
    with nc.Block() as block:
        @block.tensor
        def _(pe):
            def scores(n):
                h, b = tasks[n]
                a, e = half(h)
                if n >= 3:
                    pe.wait_ge(scaled, n - 2)
                pe.matmul(K.ps[:, n % 3, b * P:T], proj[a:e, KB + h // 2, b * P:(b + 1) * P],
                          proj[a:e, QB + h // 2, b * P:T], start=True, stop=True).then_inc(scored, 1)

            def sums(n):
                h, b = tasks[n]
                pe.wait_ge(masked, n + 1)
                if n >= 3:
                    pe.wait_ge(logged, n - 2)
                for c in range(b, QT):
                    mm = pe.matmul(K.ps[:, 3 + n % 3, c * P:T], upper if c == b else K.ones[:, :],
                                   sp[:, h % 2, c, c * P:T], start=c == b, stop=c == QT - 1)
                mm.then_inc(summed, 1)

            def value(h):
                a, e = half(h)
                pe.wait_ge(weighed, QT * (h + 1))
                if h >= 2:
                    pe.wait_ge(outed, h - 1)
                for b in range(QT):
                    mm = pe.matmul(K.ps[a:e, 6 + h % 2, b * P:T], vb[:, b, h * HD:(h + 1) * HD],
                                   z[:, h % 2, b, b * P:T], start=b == 0, stop=b == QT - 1)
                mm.then_inc(valued, 1)

            for n in range(2):
                scores(n)
            for n, (h, b) in enumerate(tasks):
                if n + 2 < len(tasks):
                    scores(n + 2)
                sums(n)
                if b == 2 and h >= 1:
                    value(h - 1)
            value(HEADS - 1)

        @block.scalar
        def _(act):
            def soften(n):
                h, b = tasks[n]
                t = tmp[:, n % 4, b * P:T]
                act.wait_ge(scored, n + 1)
                if h >= 2:
                    act.wait_ge(valued, h - 1)
                act.activation(z[:, h % 2, b, b * P:T], K.ps[:, n % 3, b * P:T], ACT.Copy,
                               scale=HD ** -0.5).then_inc(scaled, 1)
                if n >= 4:
                    act.wait_ge(masked, n - 3)
                act.wait_ge(scaled, n + 1)
                act.activation(t, z[:, h % 2, b, b * P:T], ACT.Abs).then_inc(folded, 1)
                act.wait_ge(folded, n + 1)
                act.activation(t, t, ACT.Exp, scale=-1.0).then_inc(faded, 1)
                act.wait_ge(faded, n + 1)
                act.activation(t, t, ACT.Ln, bias=1.0).then_inc(softened, 1)

            def weigh(n):
                h, b = tasks[n]
                act.wait_ge(logged, n + 1)
                act.activation(z[:, h % 2, b, b * P:T], z[:, h % 2, b, b * P:T], ACT.Exp).then_inc(weighed, 1)

            soften(0)
            for n in range(len(tasks)):
                if n + 1 < len(tasks):
                    soften(n + 1)
                weigh(n)

        @block.vector
        def _(dve):
            steps = [0]
            chain = K.sem("stick_chain")

            def link(ins):
                steps[0] += 1
                ins.then_inc(chain, 1)
                dve.wait_ge(chain, steps[0])

            def plus(n):
                h, b = tasks[n]
                dve.wait_ge(softened, n + 1)
                if h >= 2:
                    dve.wait_ge(summed, QT * (h - 1))
                s, diag = sp[:, h % 2, b, b * P:T], sp[:, h % 2, b, b * P:(b + 1) * P]
                link(dve.scalar_tensor_tensor(out=s, in0=z[:, h % 2, b, b * P:T], scalar=0.0,
                                              in1=tmp[:, n % 4, b * P:T], op0=ALU.max, op1=ALU.add))
                dve.tensor_tensor(diag, diag, s01, ALU.mult).then_inc(masked, 1)

            def out(dve, h):
                a, e = half(h)
                dve.wait_ge(valued, h + 1)
                dve.tensor_copy(o_b[a:e, 4 + h // 2, 0:T], K.ps[a:e, 6 + h % 2, :]).then_inc(outed, 1)

            plus(0)
            for n, (h, b) in enumerate(tasks):
                if n + 1 < len(tasks):
                    plus(n + 1)
                dve.wait_ge(summed, n + 1)
                zz, diag = z[:, h % 2, b, b * P:T], z[:, h % 2, b, b * P:(b + 1) * P]
                link(dve.tensor_tensor(zz, zz, K.ps[:, 3 + n % 3, b * P:T], ALU.subtract))
                dve.tensor_tensor(diag, diag, sneg, ALU.add).then_inc(logged, 1)
                if b == 0 and h >= 1:
                    out(dve, h - 1)
            out(dve, HEADS - 1)

    K.end()


def merge(K, proj):
    d = K.dram
    merged = proj

    def groups(j):
        return [(s, 0, T, P, [(K.ring[:, j, (s * 4 + k) * P:(s * 4 + k + 1) * P], K.h[:, s * 4 + k, 0:T])
                              for k in range(4)]) for s in range(2)]
    with ExitStack() as own:
        gated = own.enter_context(K.nc.sbuf_tensor("gated", [P, RING, 2, T], F32))
        both = K.sem("merge_both")
        count = [0]

        def take(dve, m, banks):
            j = count[0] % RING
            count[0] += 1
            dve.tensor_tensor(gated[:, j, 0, :], banks[0], proj[:, GA + m, :], ALU.mult)
            dve.tensor_tensor(gated[:, j, 1, :], banks[1], proj[:, GB + m, :], ALU.mult).then_inc(both, 1)
            dve.wait_ge(both, m + 1)
            return dve.tensor_tensor(merged[:, m, :], gated[:, j, 0, :], gated[:, j, 1, :], ALU.add)
        linear(K, "branches", d["w_branches"], KD, 2, groups, 1024, on_dve=take)
    residual(K, "w_out", d["w_out"], 4, merged, KD, 256, LAT)


def residual(K, name, w, panels, acts, kc, width, spans, gate=None):
    per = width // P
    n = len(spans)

    def take(dve, m, banks):
        for u in range(per):
            for s, (a, c) in enumerate(spans):
                x = K.x[:, m * per + u, a:a + c]
                if gate is None:
                    last = dve.tensor_tensor(x, banks[u * n + s][:, 0:c], x, ALU.add)
                else:
                    last = dve.scalar_tensor_tensor(out=x, in0=banks[u * n + s][:, 0:c], scalar=gate(m * per + u, s),
                                                    in1=x, op0=ALU.mult, op1=ALU.add)
        return last
    linear(K, name, w, panels, per * n, features_out(K, acts, kc, width, spans), kc * width, on_dve=take)


def route(K):
    nc, d = K.nc, K.dram
    with ExitStack() as own:
        def sb(name, *shape):
            return own.enter_context(nc.sbuf_tensor(f"route_{name}", list(shape), F32))
        w, b, logits = sb("w", P, KD, 36), sb("b", 1, 36), sb("logits", P, QT, 36)
        eq, seen, sel, top = sb("eq", P, 8), sb("seen", P, 8), sb("sel", P, 3, 8), sb("top", P, 8)
        gexp, small, gsel, esel = sb("gexp", P, 4), sb("small", P, 8), sb("gsel", P, 4), sb("esel", P, 8)
        comb, combt = sb("comb", P, QT, 32), sb("combt", 32, T)
        here, logit, ready, chain, shifted, exped = (K.sem(f"route_{n}") for n in (
            "here", "logit", "ready", "chain", "shifted", "exped"))
        combed, turned, out, stored = (K.sem(f"route_{n}") for n in ("combed", "turned", "out", "stored"))
        block = own.enter_context(nc.Block())

        @block.sync
        def _(sp):
            sp.dma_start(w[:, :, :], d["w_route"]).then_inc(here, 16)
            sp.dma_start(b[:, :], d["b_route"]).then_inc(here, 16)
            sp.wait_ge(out, 1)
            sp.dma_start(d["comb"], combt[:, :]).then_inc(stored, 16)
            sp.wait_ge(stored, 16)

        @block.tensor
        def _(pe):
            pe.wait_ge(here, 32)
            for q in range(QT):
                for k in range(KD):
                    pe.matmul(K.ps[:, q, 0:36], K.h[:, k, q * P:(q + 1) * P], w[:, k, :], start=k == 0, stop=False)
                pe.matmul(K.ps[:, q, 0:36], K.ones[0:1, 0:P], b[:, :], start=False, stop=True).then_inc(logit, 1)
            pe.wait_ge(combed, QT)
            for q in range(QT):
                mm = pe.transpose(K.ps[0:32, 4, q * P:(q + 1) * P], comb[:, q, :], K.ident[:, :])
            mm.then_inc(turned, 1)

        @block.scalar
        def _(act):
            for q in range(QT):
                act.wait_ge(shifted, 2 * q + 1)
                act.activation(gexp[:, :], logits[:, q, 0:4], ACT.Exp, bias=small[:, 0:1],
                               accum_out=small[:, 1:2]).then_inc(exped, 1)
                act.wait_ge(shifted, 2 * q + 2)
                act.activation(small[:, 4:5], small[:, 3:4], ACT.Exp).then_inc(exped, 1)

        @block.vector
        def _(dve):
            steps = [0]

            def link(ins):
                steps[0] += 1
                ins.then_inc(chain, 1)
                dve.wait_ge(chain, steps[0])

            def first_of(dst, n):
                link(dve.tensor_tensor_scan(seen[:, 0:n], K.ones[:, 0:n], eq[:, 0:n], 0.0, ALU.mult, ALU.add))
                link(dve.scalar_tensor_tensor(out=dst, in0=seen[:, 0:n], scalar=1.0, in1=eq[:, 0:n],
                                              op0=ALU.is_equal, op1=ALU.mult))

            for q in range(QT):
                dve.wait_ge(logit, q + 1)
                link(dve.tensor_copy(logits[:, q, :], K.ps[:, q, 0:36]))
                g, e = logits[:, q, 0:4], logits[:, q, 4:36]
                link(dve.reduce_max(small[:, 2:3], g, AX))
                dve.tensor_scalar(small[:, 0:1], small[:, 2:3], -1.0, None, ALU.mult).then_inc(shifted, 1)
                link(dve.tensor_scalar(eq[:, 0:4], g, small[:, 2:3], None, ALU.is_equal))
                first_of(gsel[:, :], 4)
                link(dve.tensor_scalar(esel[:, :], e[:, 0:8], gsel[:, 0:1], None, ALU.mult))
                for n in range(1, 4):
                    link(dve.scalar_tensor_tensor(out=esel[:, :], in0=e[:, 8 * n:8 * n + 8], scalar=gsel[:, n:n + 1],
                                                  in1=esel[:, :], op0=ALU.mult, op1=ALU.add))
                link(dve.max(top[:, :], esel[:, :]))
                dve.tensor_tensor(small[:, 3:4], top[:, 1:2], top[:, 0:1], ALU.subtract).then_inc(shifted, 1)
                link(dve.tensor_scalar(eq[:, :], esel[:, :], top[:, 0:1], None, ALU.is_equal))
                first_of(sel[:, 0, :], 8)
                link(dve.scalar_tensor_tensor(out=eq[:, :], in0=esel[:, :], scalar=top[:, 1:2], in1=sel[:, 0, :],
                                              op0=ALU.is_equal, op1=ALU.is_gt))
                first_of(sel[:, 1, :], 8)
                dve.wait_ge(exped, 2 * q + 2)
                link(dve.tensor_scalar(small[:, 5:6], small[:, 4:5], 1.0, small[:, 1:2], ALU.add, ALU.mult))
                link(dve.reciprocal(small[:, 6:7], small[:, 5:6]))
                link(dve.tensor_scalar(sel[:, 2, :], sel[:, 1, :], small[:, 4:5], None, ALU.mult))
                link(dve.tensor_tensor(sel[:, 2, :], sel[:, 2, :], sel[:, 0, :], ALU.add))
                link(dve.tensor_scalar(sel[:, 2, :], sel[:, 2, :], small[:, 6:7], None, ALU.mult))
                for n in range(4):
                    ins = dve.tensor_scalar(comb[:, q, 8 * n:8 * n + 8], sel[:, 2, :], gsel[:, n:n + 1], None, ALU.mult)
                ins.then_inc(combed, 1)
            dve.wait_ge(turned, 1)
            dve.tensor_copy(combt[:, :], K.ps[0:32, 4, :]).then_inc(out, 1)
    K.end()


def experts(K):
    nc, d = K.nc, K.dram
    with ExitStack() as own:
        weights = own.enter_context(nc.sbuf_tensor("expert_weights", [P, 2, 3, KD * 256], F32))
        share = own.enter_context(nc.sbuf_tensor("expert_share", [P, 2, T], F32))
        silu = own.enter_context(nc.sbuf_tensor("expert_silu", [P, 2, T], F32))
        hid = own.enter_context(nc.sbuf_tensor("expert_hidden", [P, 2, 2, T], F32))
        up_here = [K.sem(f"moe_up_here{u}") for u in range(2)]
        down_here = [K.sem(f"moe_down_here{u}") for u in range(2)]
        upped = [K.sem(f"moe_upped{u}") for u in range(2)]
        downed = [K.sem(f"moe_downed{u}") for u in range(2)]
        silued, rose, mixed = K.sem("moe_silued"), K.sem("moe_rose"), [K.sem(f"moe_mixed{u}") for u in range(2)]
        added = [K.sem(f"moe_added{u}") for u in range(2)]
        block = own.enter_context(nc.Block())

        @block.sync
        def _(sp):
            with sp.Fori(0, N_EXP // 2) as i:
                for u in range(2):
                    e = i * 2 + u
                    sp.wait_ge(upped[u], i * 2 + 1)
                    for n, name in enumerate(("w_gate", "w_up")):
                        sp.dma_start(weights[:, u, n, :], d[name][e]).then_inc(up_here[u], 16)
                    sp.wait_ge(downed[u], i * 8 + 1)
                    sp.dma_start(weights[:, u, 2, :], d["w_down"][e]).then_inc(down_here[u], 16)
                    sp.wait_ge(mixed[u], i * 2 + 1)
                    sp.dma_start(share[:, u, :], d["comb"][ds(e, 1), :].to_broadcast([P, T])).then_inc(down_here[u], 16)

        @block.tensor
        def _(pe):
            def up(i, u, waits):
                pe.wait_ge(up_here[u], (i + 1) * 32)
                for f in range(2):
                    if waits is not None:
                        pe.wait_ge(mixed[1 - u], waits(f) + 1)
                    for n in range(2):
                        for k in range(KD):
                            mm = pe.matmul(K.ps[:, 2 * n + f, :], weights[:, u, n, k * 256 + f * P:k * 256 + (f + 1) * P],
                                           K.h[:, k, 0:T], start=k == 0, stop=k == KD - 1)
                    mm.then_inc(upped[u], 1)

            def down(i, u, before):
                pe.wait_ge(down_here[u], (i + 1) * 32)
                pe.wait_ge(mixed[u], (i + 1) * 2 + 1)
                for m in range(KD):
                    if m >= 4:
                        pe.wait_ge(added[u], i * 8 + m - 3)
                    elif before is not None:
                        pe.wait_ge(added[1 - u], before + m)
                    for f in range(2):
                        mm = pe.matmul(K.ps[:, 4 + m % 4, :], weights[:, u, 2, f * D + m * P:f * D + (m + 1) * P],
                                       hid[:, u, f, :], start=f == 0, stop=f == 1)
                    mm.then_inc(downed[u], 1)

            for u in range(2):
                pe.sem_inc(upped[u], 1)
                pe.sem_inc(downed[u], 1)
            up(0, 0, None)
            up(0, 1, lambda f: f + 1)
            down(0, 0, None)
            with pe.Fori(1, N_EXP // 2) as i:
                up(i, 0, lambda f: i * 2 + f - 1)
                down(i - 1, 1, (i - 1) * 8 + 5)
                up(i, 1, lambda f: i * 2 + f + 1)
                down(i, 0, (i - 1) * 8 + 5)
            down(N_EXP // 2 - 1, 1, (N_EXP // 2 - 1) * 8 + 5)

        @block.scalar
        def _(act):
            with act.Fori(0, N_EXP // 2) as i:
                for u in range(2):
                    for f in range(2):
                        act.wait_ge(upped[u], i * 2 + f + 1 + 1)
                        if u:
                            act.wait_ge(mixed[0], i * 2 + f + 1 + 1)
                        else:
                            act.wait_ge(mixed[1], i * 2 + 1)
                        act.activation(silu[:, f, :], K.ps[:, f, :], ACT.Silu).then_inc(silued, 1)

        @block.vector
        def _(dve):
            def mix(i, u, first):
                for f in range(2):
                    n = i * 4 + u * 2 + f
                    dve.wait_ge(silued, n + 1)
                    if not first:
                        dve.wait_ge(downed[u], i * 8 + 1)
                    dve.tensor_tensor(hid[:, u, f, :], K.ps[:, 2 + f, :], silu[:, f, :], ALU.mult).then_inc(rose, 1)
                    dve.wait_ge(down_here[u], (i + 1) * 32)
                    dve.wait_ge(rose, n + 1)
                    dve.tensor_tensor(hid[:, u, f, :], hid[:, u, f, :], share[:, u, :], ALU.mult).then_inc(mixed[u], 1)

            def add(i, u):
                for m in range(KD):
                    dve.wait_ge(downed[u], i * 8 + m + 1 + 1)
                    dve.tensor_tensor(K.x[:, m, 0:T], K.ps[:, 4 + m % 4, :], K.x[:, m, 0:T],
                                      ALU.add).then_inc(added[u], 1)

            for u in range(2):
                dve.sem_inc(mixed[u], 1)
            mix(0, 0, True)
            mix(0, 1, True)
            add(0, 0)
            with dve.Fori(1, N_EXP // 2) as i:
                mix(i, 0, False)
                add(i - 1, 1)
                mix(i, 1, False)
                add(i, 0)
            add(N_EXP // 2 - 1, 1)
    K.end()


def embed_gate(K):
    nc, d = K.nc, K.dram
    with ExitStack() as own:
        p = own.enter_context(nc.sbuf_tensor("ple", [P, 2, T], F32))
        gate = own.enter_context(nc.sbuf_tensor("ple_gate", [P, RING, T], F32))
        gated = own.enter_context(nc.sbuf_tensor("ple_gated", [P, RING, T], F32))
        load(K, "load_p", [(p[:, :, :], d["p"])])
        own_product = K.sem("ple_product")

        def groups(j):
            return [(0, 0, T, P, [(K.ring[:, j, k * P:(k + 1) * P], K.h[:, k, 0:T]) for k in range(KD)]),
                    (1, 0, T, P, [(K.ring[:, j, (KD + k) * P:(KD + k + 1) * P], p[:, k, :]) for k in range(2)])]
        turn = {"act": 0, "dve": 0}

        def sigmoid(act, m, banks):
            u = turn["act"] % RING
            turn["act"] += 1
            return act.activation(gate[:, u, :], banks[0], ACT.Sigmoid)

        def take(dve, m, banks):
            u = turn["dve"] % RING
            turn["dve"] += 1
            dve.tensor_tensor(gated[:, u, :], gate[:, u, :], banks[1], ALU.mult).then_inc(own_product, 1)
            dve.wait_ge(own_product, m + 1)
            return dve.tensor_tensor(K.x[:, m, 0:T], K.x[:, m, 0:T], gated[:, u, :], ALU.add)
        linear(K, "ple", d["w_ple"], KD, 2, groups, 10 * P, on_act=sigmoid, on_dve=take)


def first_block(K):
    nc, d = K.nc, K.dram
    norm_model(K, "attn_norm", LAT, lambda i, k: K.v("attn_norm", k))
    with ExitStack() as own:
        proj = own.enter_context(nc.sbuf_tensor("projected", [P, 34, T], F32))
        vb = own.enter_context(nc.sbuf_tensor("v_b", [P, QT, 512], F32))
        widx = own.enter_context(nc.sbuf_tensor("w_idx", [P, QT * 8], F32))
        masks = own.enter_context(nc.sbuf_tensor("masks", [P, 4, P], F32))
        load(K, "load_masks", [(masks[:, :, :], d["masks"])])
        K.bias = K.flat[:, 12 * T:20 * T].rearrange("p (h n) -> p h n", h=HEADS)
        project_in(K, proj, vb, widx)
        sparse_attention(K, proj, widx, masks[:, 0, :])
        stick_breaking(K, proj, vb, masks[:, 1, :], masks[:, 2, :], masks[:, 3, :])
        merge(K, proj)
    norm_model(K, "ffn_norm", LAT, lambda i, k: K.v("ffn_norm", k))
    route(K)
    experts(K)
    norm_model(K, "ple_norm", LAT, lambda i, k: K.v("ple_norm", k))
    embed_gate(K)
    rms(K, "final_norm", [([K.x[:, k, 0:T] for k in range(KD)], [K.x[:, k, 0:T] for k in range(KD)], T)], D,
        lambda i, k: K.v("final_norm", k))



SHIFT1, SCALE1, GATE1, SHIFT2, SCALE2, GATE2 = (KD * n for n in range(6))


def modulations(K):
    nc, d = K.nc, K.dram
    with ExitStack() as own:
        cs = own.enter_context(nc.sbuf_tensor("silu_c", [P, KD, 2], F32))
        with nc.Block() as block:
            @block.scalar
            def _(act):
                for s, name in enumerate(("c_lat", "c_ctx")):
                    at = VEC_AT[name][0]
                    act.activation(cs[:, :, s], K.vec[:, at:at + KD], ACT.Silu)

        def groups(j):
            return [(0, w * 2, 2, P, [(K.ring[:, j, k * 256 + w * P:k * 256 + (w + 1) * P], cs[:, k, :])
                                      for k in range(KD)]) for w in range(2)]
        for layer in range(2):
            def take(dve, m, banks, layer=layer):
                for w in range(2):
                    at = VEC_AT[f"b_ada_{layer}"][0]
                    last = dve.tensor_scalar(K.mod[:, layer, m * 2 + w, :], banks[0][:, w * 2:w * 2 + 2],
                                             K.vec[:, ds(m * 2 + (at + w), 1)], None, ALU.add)
                return last
            linear(K, f"ada{layer}", d[f"ada_{layer}"], 24, 2, groups, 2048, on_dve=take)
    with nc.Block() as block:
        @block.vector
        def _(dve):
            for layer in range(2):
                for n, scale in enumerate((SCALE1, SCALE2)):
                    at = VEC_AT[f"norm{n + 1}_{layer}"][0]
                    dve.scalar_tensor_tensor(out=K.gain[:, layer, n, :, :], in0=K.mod[:, layer, scale:scale + KD, :],
                                             scalar=1.0, op0=ALU.add, op1=ALU.mult,
                                             in1=K.vec[:, at:at + KD].unsqueeze(2).to_broadcast([P, KD, 2]))


def norm_modulated(K, layer, n, spans):
    shift = (SHIFT1, SHIFT2)[n]
    norm_model(K, f"norm{n}_{layer}", spans, lambda i, k: K.gain[:, layer, n, k, i:i + 1],
               lambda i, k: K.mod[:, layer, shift + k, i:i + 1])


def feed_forward(K, layer, spans):
    n = len(spans)
    norm_modulated(K, layer, 1, spans)
    with ExitStack() as own:
        hid = own.enter_context(K.nc.sbuf_tensor(f"ff_hidden{layer}", [P, KF, N], F32))
        silu = own.enter_context(K.nc.sbuf_tensor(f"ff_silu{layer}", [P, RING, N], F32))
        turn = {"act": 0, "dve": 0}

        def gate(act, m, banks):
            j = turn["act"] % RING
            turn["act"] += 1
            for s, (a, c) in enumerate(spans):
                last = act.activation(silu[:, j, a:a + c], banks[s][:, 0:c], ACT.Silu)
            return last

        def take(dve, m, banks):
            j = turn["dve"] % RING
            turn["dve"] += 1
            for s, (a, c) in enumerate(spans):
                last = dve.tensor_tensor(hid[:, m, a:a + c], banks[n + s][:, 0:c], silu[:, j, a:a + c], ALU.mult)
            return last
        linear(K, f"ff_up{layer}", K.dram[f"w13_{layer}"], KF, 2 * n, features_out(K, K.h, KD, 256, spans), 2048,
               on_act=gate, on_dve=take)
        residual(K, f"ff_down{layer}", K.dram[f"w2_{layer}"], KD, hid, KF, P, spans,
                 lambda k, s: K.mod[:, layer, k + GATE2, s:s + 1])


def rotate(K, pairs, cos, sin, rot):
    nc = K.nc
    made, spun, sined, cosed = (K.sem(f"rope_{n}") for n in ("made", "spun", "sined", "cosed"))
    with ExitStack() as own:
        tmp = own.enter_context(nc.sbuf_tensor("rope_tmp", [64, 2, T], F32))
        block = own.enter_context(nc.Block())

        @block.tensor
        def _(pe):
            for n, t in enumerate(pairs):
                if n >= 4:
                    pe.wait_ge(sined, n - 3)
                pe.matmul(K.ps[0:64, n % 4, :], rot, t, start=True, stop=True).then_inc(made, 1)

        @block.vector
        def _(dve):
            for n, t in enumerate(pairs):
                dve.wait_ge(made, n + 1)
                dve.tensor_tensor(tmp[:, n % 2, :], K.ps[0:64, n % 4, :], sin, ALU.mult).then_inc(sined, 1)
                dve.tensor_tensor(t, t, cos, ALU.mult).then_inc(cosed, 1)
                dve.wait_ge(sined, n + 1)
                dve.wait_ge(cosed, n + 1)
                dve.tensor_tensor(t, t, tmp[:, n % 2, :], ALU.add)
    K.end()


def latent_attention(K):
    nc, d = K.nc, K.dram
    norm_modulated(K, 0, 0, BOTH)
    with ExitStack() as own:
        low = own.enter_context(nc.sbuf_tensor("low_rank", [P, 6, N], F32))
        qn = own.enter_context(nc.sbuf_tensor("q_nope", [P, HEADS, N], F32))
        qr = own.enter_context(nc.sbuf_tensor("q_rope", [64, HEADS, N], F32))
        v = own.enter_context(nc.sbuf_tensor("values", [P, N // P, HEADS * P], F32))
        rope = own.enter_context(nc.sbuf_tensor("rope", [64, 2, T], F32))
        rot = own.enter_context(nc.sbuf_tensor("rot", [64, 64], F32))
        kr = low[0:64, 5, :]

        def take(dve, m, banks):
            for s, (a, c) in enumerate(BOTH):
                last = dve.tensor_copy(low[:, m, a:a + c], banks[s][:, 0:c])
            return last
        linear(K, "mla_in", d["mla_in"], 5, 2, features_out(K, K.h, KD, P, BOTH), KD * P, on_dve=take)

        def rope_out(j):
            return [(s, 0, c, 64, [(K.ring[:, j, k * 64:(k + 1) * 64], K.h[:, k, a:a + c]) for k in range(KD)])
                    for s, (a, c) in enumerate(BOTH)]

        def take_rope(dve, m, banks):
            for s, (a, c) in enumerate(BOTH):
                last = dve.tensor_copy(kr[:, a:a + c], banks[s][0:64, 0:c])
            return last
        linear(K, "mla_in_rope", d["mla_in_rope"], 1, 2, rope_out, KD * 64, on_dve=take_rope)
        load(K, "load_rope", [(rope[:, :, :], d["rope"]), (rot[:, :], d["rot"])])

        def chunks(ap, which, rows=P):
            return [([ap[0:rows, k, a:a + c] for k in which], [ap[0:rows, k, a:a + c] for k in which], c)
                    for a, c in BOTH]
        rms(K, "mla_q_norm", chunks(low, range(3)), 384, lambda i, k: K.v("q_norm", k))
        rms(K, "mla_kv_norm", chunks(low, (3, 4)), 256, lambda i, k: K.v("mkv_norm", k))
        rms(K, "mla_kr_norm", chunks(low, (5,), 64), 64, lambda i, k: K.v("kr", 0, 64), rows=64)
        kn = K.h

        def q_out(j):
            out = []
            for s, (a, c) in enumerate(BOTH):
                out.append((s, 0, c, P, [(K.ring[:, j, k * 192:k * 192 + P], low[:, k, a:a + c]) for k in range(3)]))
                out.append((2 + s, 0, c, 64, [(K.ring[:, j, k * 192 + P:(k + 1) * 192], low[:, k, a:a + c])
                                              for k in range(3)]))
            return out

        def take_qr(act, m, banks):
            for s, (a, c) in enumerate(BOTH):
                last = act.activation(qr[:, m, a:a + c], banks[2 + s][0:64, 0:c], ACT.Copy)
            return last

        def take_qn(dve, m, banks):
            for s, (a, c) in enumerate(BOTH):
                last = dve.tensor_copy(qn[:, m, a:a + c], banks[s][:, 0:c])
            return last
        linear(K, "mla_q", d["mla_uq"], HEADS, 4, q_out, 576, on_act=take_qr, on_dve=take_qn)

        def kv_out(j):
            out = [(s, 0, c, P, [(K.ring[:, j, k * 256:k * 256 + P], low[:, 3 + k, a:a + c]) for k in range(2)])
                   for s, (a, c) in enumerate(BOTH)]
            return out + [(2 + t // 4, (t % 4) * P, P, P,
                           [(low[:, 3 + k, t * P:(t + 1) * P], K.ring[:, j, k * 256 + P:(k + 1) * 256])
                            for k in range(2)]) for t in range(N // P)]

        def take_v(act, m, banks):
            for b, t, n in ((2, 0, 4), (3, 4, 2)):
                last = act.activation(v[:, t:t + n, ds(m * P, P)],
                                      banks[b][:, 0:n * P].rearrange("p (t e) -> p t e", t=n), ACT.Copy)
            return last

        def take_kn(dve, m, banks):
            for s, (a, c) in enumerate(BOTH):
                last = dve.tensor_copy(kn[:, m, a:a + c], banks[s][:, 0:c])
            return last
        linear(K, "mla_kv", d["mla_ukv"], HEADS, 4, kv_out, 512, on_act=take_v, on_dve=take_kn)

        def heads(ap, rows=P):
            return [([ap[0:rows, h, a:a + c]], [ap[0:rows, h, a:a + c]], c) for h in range(HEADS) for a, c in BOTH]
        rms(K, "mla_qn", heads(qn), P, lambda i, k: K.v("qn"))
        rms(K, "mla_kn", heads(kn), P, lambda i, k: K.v("kn"))
        rms(K, "mla_qr", heads(qr, 64), 64, lambda i, k: K.v("qr", 0, 64), rows=64)
        rotate(K, [qr[:, h, 0:T] for h in range(HEADS)] + [kr[:, 0:T]], rope[:, 0, :], rope[:, 1, :], rot[:, :])

        tasks = []
        for h in range(HEADS):
            for i in range(N // P):
                k0 = 0 if i < QT else QT
                q = slice(i * P, (i + 1) * P)
                tasks.append((h, N - k0 * P, [(qn[:, h, q], kn[:, h, k0 * P:N]), (qr[:, h, q], kr[:, k0 * P:N])],
                              k0, i * P, None, None))

        def values(h, turn):
            vh = [v[:, t, h * P:(h + 1) * P] for t in range(N // P)]
            return [(6, 0, T, [(vh[t], turn[:, t, 0:T], 0) for t in range(N // P)]),
                    (7, 0, C, [(vh[t], turn[:, t, T:N], 0) for t in range(QT, N // P)])]
        attend(K, "mla", tasks, (N // P, N, N), HEADS, 192 ** -0.5, values,
               lambda h: [(qn[:, h, 0:T], 6, T), (qn[:, h, T:N], 7, C)])
        residual(K, "mla_out", d["mla_out"], 4, qn, KD, 256, BOTH, lambda k, s: K.mod[:, 0, k + GATE1, s:s + 1])


LEVELS = 7
CH = N // P
ORDER = ([4, 5, 0, 1, 2, 3], [5, 4, 3, 2, 1, 0])
LAST = (P - 1, 0)


def recurrence(K, sig, q, inp, lb, masks):
    nc = K.nc
    f = K.flat
    at = [0]

    def part(n):
        at[0] += n
        return f[:, at[0] - n:at[0]]
    kp = [part(N) for _ in range(2)]
    dec = [part(N) for _ in range(2)]
    key = [part(N) for _ in range(2)]
    qd = [part(T) for _ in range(2)]
    att = [part(T).rearrange("p (c t) -> p c t", c=QT) for _ in range(2)]
    state = [part(4 * P).rearrange("p (c t) -> p c t", c=4) for _ in range(2)]
    knat = [part(5 * P).rearrange("p (c t) -> p c t", c=5) for _ in range(2)]
    vh = part(N).rearrange("p (c t) -> p c t", c=CH)
    lev = K.h[:, :, :].rearrange("p k n -> p (k n)")[:, 0:LEVELS * T].rearrange("p (l n) -> p l n", l=LEVELS)
    names = ("f", "ln", "scan", "key", "lastdiff", "lastexp", "qexp", "kprime", "qdec", "turned", "knat", "diffed",
             "exped", "grown", "product", "picked", "stated", "spread", "valued", "outed", "vcopied", "zeroed", "clear")
    S = {n: K.sem(f"hg_{n}") for n in names}
    STEPS, PRODUCTS, STATES = 2 * LEVELS, 2 * (LEVELS + 1), 10

    def halves(ap, l):
        v = ap.rearrange("p (b s n) -> p b s n", s=2, n=P >> (l + 1))
        return v

    def sides(ap, l, r):
        v = halves(ap, l)
        return (v[:, :, 1, :], v[:, :, 0, :]) if r == 0 else (v[:, :, 0, :], v[:, :, 1, :])

    def middle(ap, l, r):
        n = P >> (l + 1)
        v = halves(ap, l)
        m = v[:, :, 0, n - 1:n] if r == 0 else v[:, :, 1, 0:1]
        return m.to_broadcast([P, T >> (LEVELS - l), n])

    with ExitStack() as own:
        elast = own.enter_context(nc.sbuf_tensor("hg_elast", [P, 2, CH], F32))
        block = own.enter_context(nc.Block())

        @block.gpsimd
        def _(pool):
            for n in ("lastdiff", "diffed"):
                pool.sem_inc(S[n], 1)
            with pool.Fori(0, HEADS) as i:
                for r in range(2):
                    pool.wait_ge(S["scan"], i * 2 + r + 1 + 1)
                    d3 = dec[r].rearrange("p (c t) -> p c t", c=CH)
                    pool.tensor_tensor(kp[r].rearrange("p (c t) -> p c t", c=CH),
                                       d3[:, :, LAST[r]:LAST[r] + 1].to_broadcast([P, CH, P]), d3,
                                       ALU.subtract).then_inc(S["lastdiff"], 1)
                    for l in range(LEVELS):
                        pool.wait_ge(S["product"], i * PRODUCTS + (l + 2 if r else 0) + 1)
                        dq, dk = sides(dec[r][:, 0:T], l, r)
                        eq, ek = sides(lev[:, l, :], l, r)
                        pool.tensor_tensor(eq, dq, middle(dec[r][:, 0:T], l, r), ALU.subtract)
                        pool.tensor_tensor(ek, middle(dec[r][:, 0:T], l, r), dk, ALU.subtract).then_inc(S["diffed"], 1)

        @block.scalar
        def _(act):
            for n in ("ln", "qexp", "lastexp", "exped", "knat", "outed", "vcopied"):
                act.sem_inc(S[n], 1)
            with act.Fori(0, HEADS) as i:
                act.wait_ge(S["valued"], i + 1)
                act.activation(vh, inp[:, :, ds(i * P, P)], ACT.Copy).then_inc(S["vcopied"], 1)
                for r in range(2):
                    act.wait_ge(S["f"], i * 2 + r + 1 + 1)
                    act.activation(kp[r], kp[r], ACT.Ln).then_inc(S["ln"], 1)
                for r in range(2):
                    act.wait_ge(S["scan"], i * 2 + r + 1 + 1)
                    act.activation(qd[r], dec[r][:, 0:T], ACT.Exp)
                    act.activation(elast[:, r, :], dec[r].rearrange("p (c t) -> p c t", c=CH)[:, :, LAST[r]],
                                   ACT.Exp).then_inc(S["qexp"], 1)
                    act.wait_ge(S["lastdiff"], i * 2 + r + 1 + 1)
                    act.activation(kp[r], kp[r], ACT.Exp).then_inc(S["lastexp"], 1)
                    for l in range(LEVELS):
                        act.wait_ge(S["diffed"], i * STEPS + r * LEVELS + l + 1 + 1)
                        act.activation(lev[:, l, :], lev[:, l, :], ACT.Exp).then_inc(S["exped"], 1)
                    act.wait_ge(S["turned"], i * 2 + r + 1 + 1)
                    act.activation(knat[r].rearrange("p c t -> p (c t)"), K.psf[:, 4 * BANK:4 * BANK + 5 * P],
                                   ACT.Copy).then_inc(S["knat"], 1)
                act.wait_ge(S["valued"], i + 1 + 1)
                act.activation(q[:, i, :], K.ps[:, 7, :], ACT.Copy).then_inc(S["outed"], 1)

        @block.tensor
        def _(pe):
            def states(i, r):
                pe.wait_ge(S["vcopied"], i + 1 + 1)
                pe.wait_ge(S["knat"], i * 2 + r + 1 + 1)
                pe.wait_ge(S["spread"], i * STATES + r * 5 + 1)
                pe.wait_ge(S["outed"], i + 1)
                for n in range(5):
                    mm = pe.matmul(K.psf[:, 6 * BANK + n * P:6 * BANK + (n + 1) * P], knat[r][:, n, :],
                                   vh[:, ORDER[r][n], :], start=True, stop=True)
                mm.then_inc(S["stated"], 1)

            for n in ("turned", "product", "stated", "valued"):
                pe.sem_inc(S[n], 1)
            with pe.Fori(0, HEADS) as i:
                for r in range(2):
                    p0 = r * (LEVELS + 1)
                    pe.wait_ge(S["key"], i * 2 + r + 1 + 1)
                    pe.wait_ge(S["picked"], i * PRODUCTS + max(p0 - 3, 0) + 1)
                    for c in range(QT):
                        mm = pe.matmul(K.ps[:, p0 % 4, c * P:(c + 1) * P], key[r][:, c * P:(c + 1) * P],
                                       q[:, i, c * P:(c + 1) * P], start=True, stop=True)
                    mm.then_inc(S["product"], 1)
                    pe.wait_ge(S["kprime"], i * 2 + r + 1 + 1)
                    pe.wait_ge(S["knat"], i * 2 + r + 1)
                    for n in range(5):
                        c = ORDER[r][n]
                        mm = pe.transpose(K.psf[:, 4 * BANK + n * P:4 * BANK + (n + 1) * P],
                                          kp[r][:, c * P:(c + 1) * P], K.ident[:, :])
                    mm.then_inc(S["turned"], 1)
                    for l in range(LEVELS):
                        p = p0 + 1 + l
                        pe.wait_ge(S["grown"], i * STEPS + r * LEVELS + l + 1 + 1)
                        pe.wait_ge(S["picked"], i * PRODUCTS + max(p - 3, 0) + 1)
                        for c in range(QT):
                            g = lev[:, l, c * P:(c + 1) * P]
                            mm = pe.matmul(K.ps[:, p % 4, c * P:(c + 1) * P], g, g, start=True, stop=True)
                        mm.then_inc(S["product"], 1)
                    states(i, r)
                pe.wait_ge(S["picked"], (i + 1) * PRODUCTS + 1)
                pe.wait_ge(S["spread"], (i + 1) * STATES + 1)
                pe.wait_ge(S["outed"], i + 1)
                pe.wait_ge(S["qdec"], (i + 1) * 2 + 1)
                for c in range(QT):
                    terms = []
                    for r in range(2):
                        terms.append((vh[:, c, :], att[r][:, c, :]))
                        terms.append((state[r][:, ORDER[r].index(c) - 2, :], qd[r][:, c * P:(c + 1) * P]))
                    for t, (a, b) in enumerate(terms):
                        mm = pe.matmul(K.ps[:, 7, c * P:(c + 1) * P], a, b, start=t == 0, stop=t == 3)
                mm.then_inc(S["valued"], 1)

        @block.vector
        def _(dve):
            for r in range(2):
                dve.memset(att[r].rearrange("p c t -> p (c t)"), 0.0).then_inc(S["zeroed"], 1)
            dve.wait_ge(S["zeroed"], 2)
            for n in ("f", "scan", "key", "kprime", "qdec", "grown", "picked", "spread"):
                dve.sem_inc(S[n], 1)
            with dve.Fori(0, HEADS) as i:
                for r in range(2):
                    dve.wait_ge(S["turned"], i * 2 + 1)
                    dve.tensor_scalar(kp[r], sig[:, r * HEADS + i, :], lb[:, 1, ds(i + r * HEADS, 1)],
                                      lb[:, 0, ds(i + r * HEADS, 1)], ALU.mult, ALU.add).then_inc(S["f"], 1)
                for r in range(2):
                    dve.wait_ge(S["ln"], i * 2 + r + 1 + 1)
                    dve.wait_ge(S["diffed"], i * STEPS + 1)
                    dve.wait_ge(S["qexp"], i * 2 + 1)
                    for c in range(CH):
                        step = slice(c * P, (c + 1) * P)
                        d, lf = dec[r][:, step], kp[r][:, step]
                        if r:
                            d, lf = d[:, ::-1], lf[:, ::-1]
                        ins = dve.tensor_tensor_scan(d, K.ones[:, :], lf, 0.0, ALU.mult, ALU.add)
                    ins.then_inc(S["scan"], 1)
                    dve.wait_ge(S["product"], i * PRODUCTS + 1)
                    dve.tensor_scalar(key[r], sig[:, r * HEADS + i, :], lb[:, 2, ds(i + r * HEADS, 1)],
                                      lb[:, 1, ds(i + r * HEADS, 1)], ALU.mult, ALU.add).then_inc(S["key"], 1)
                for r in range(2):
                    dve.wait_ge(S["lastexp"], i * 2 + r + 1 + 1)
                    dve.wait_ge(S["key"], i * 2 + r + 1 + 1)
                    dve.tensor_tensor(kp[r], kp[r], key[r], ALU.mult).then_inc(S["kprime"], 1)
                    dve.tensor_tensor(qd[r], qd[r], q[:, i, :], ALU.mult).then_inc(S["qdec"], 1)

                    def grow(l):
                        dve.wait_ge(S["exped"], i * STEPS + r * LEVELS + l + 1 + 1)
                        eq, ek = sides(lev[:, l, :], l, r)
                        qq, _ = sides(q[:, i, :], l, r)
                        _, kk = sides(key[r][:, 0:T], l, r)
                        dve.tensor_tensor(eq, eq, qq, ALU.mult)
                        dve.tensor_tensor(ek, ek, kk, ALU.mult).then_inc(S["grown"], 1)

                    def pick(p):
                        dve.wait_ge(S["product"], i * PRODUCTS + r * (LEVELS + 1) + p + 1 + 1)
                        dve.wait_ge(S["picked"], i * PRODUCTS + r * (LEVELS + 1) + p + 1)
                        dve.sem_inc(S["clear"], 1)
                        mask = masks[:, r, p, :].unsqueeze(1).to_broadcast([P, QT, P])
                        dve.copy_predicated(att[r], mask, K.ps[:, (r * (LEVELS + 1) + p) % 4, :].rearrange(
                            "p (c t) -> p c t", c=QT)).then_inc(S["picked"], 1)

                    dve.wait_ge(S["valued"], i + 1)
                    grow(0)
                    pick(0)
                    for l in range(LEVELS):
                        if l + 1 < LEVELS:
                            grow(l + 1)
                        pick(l + 1)
                    for n in range(5):
                        c = ORDER[r][n]
                        m = max(n - 1, 0)
                        product = K.psf[:, 6 * BANK + n * P:6 * BANK + (n + 1) * P]
                        dve.wait_ge(S["stated"], i * 2 + r + 1 + 1)
                        if n:
                            dve.wait_ge(S["spread"], i * STATES + r * 5 + n + 1)
                            src = state[r][:, max(n - 2, 0), :]
                            dve.scalar_tensor_tensor(out=state[r][:, m, :], in0=src, scalar=elast[:, r, c:c + 1],
                                                     in1=product, op0=ALU.mult, op1=ALU.add).then_inc(S["spread"], 1)
                        else:
                            dve.tensor_copy(state[r][:, 0, :], product).then_inc(S["spread"], 1)
    K.end()


def gated_recurrence(K):
    nc, d = K.nc, K.dram
    norm_modulated(K, 1, 0, BOTH)
    with ExitStack() as own:
        sig = own.enter_context(nc.sbuf_tensor("hg_sigmoid", [P, 2 * HEADS, N], F32))
        q = own.enter_context(nc.sbuf_tensor("hg_q", [P, HEADS, T], F32))
        g = own.enter_context(nc.sbuf_tensor("hg_gate", [P, HEADS, T], F32))
        inp = own.enter_context(nc.sbuf_tensor("hg_input", [P, CH, D], F32))
        lb = own.enter_context(nc.sbuf_tensor("hg_lb", [P, 3, 2 * HEADS], F32))
        masks = own.enter_context(nc.sbuf_tensor("hg_masks", [P, 2, LEVELS + 1, P], mybir.dt.uint32))
        load(K, "load_levels", [(masks[:, :, :, :], d["levels"])])
        a0, a1 = VEC_AT["lb0_f"][0], VEC_AT["lb1_f"][0]
        subbed = K.sem("lb_sub")
        sided = K.sem("lb_side")
        with nc.Block() as block:
            @block.vector
            def _(dve):
                dve.tensor_tensor(lb[:, 2, :], K.vec[:, a1:a1 + 2 * HEADS], K.vec[:, a0:a0 + 2 * HEADS],
                                  ALU.subtract).then_inc(subbed, 1)
                dve.wait_ge(sided, 2)
                dve.tensor_scalar(lb[:, 2, :], lb[:, 1, :], -1.0, None, ALU.mult)

            @block.scalar
            def _(act):
                act.wait_ge(subbed, 1)
                act.activation(lb[:, 0, :], lb[:, 2, :], ACT.Sigmoid).then_inc(sided, 1)
                act.activation(lb[:, 1, :], lb[:, 2, :], ACT.Sigmoid, scale=-1.0).then_inc(sided, 1)
        K.end()

        def sigmoids(act, m, banks):
            for u in range(2):
                for s, (a, c) in enumerate(BOTH):
                    last = act.activation(sig[:, m * 2 + u, a:a + c], banks[u * 2 + s][:, 0:c], ACT.Sigmoid)
            return last
        linear(K, "hg_z", d["hg_in"], 8, 4, features_out(K, K.h, KD, 256, BOTH), 2048, on_act=sigmoids)
        lat = features_out(K, K.h, KD, 256, LAT)
        linear(K, "hg_q", d["hg_in"], 4, 2, lat, 2048, on_dve=copy_pair(q), first=8)

        def silus(act, m, banks):
            act.activation(g[:, m * 2, :], banks[0], ACT.Silu)
            return act.activation(g[:, m * 2 + 1, :], banks[1], ACT.Silu)
        linear(K, "hg_g", d["hg_in"], 4, 2, lat, 2048, on_act=silus, first=12)

        def tokens_out(j):
            return [(t // 2, (t % 2) * 256, 256, P,
                     [(K.h[:, k, t * P:(t + 1) * P], K.ring[:, j, k * 256:(k + 1) * 256]) for k in range(KD)])
                    for t in range(CH)]

        def take_i(dve, m, banks):
            for t in range(CH):
                last = dve.tensor_copy(inp[:, t, ds(m * 256, 256)], banks[t // 2][:, (t % 2) * 256:(t % 2 + 1) * 256])
            return last
        linear(K, "hg_i", d["hg_in"], 4, 3, tokens_out, 2048, on_dve=take_i, first=16)
        recurrence(K, sig, q, inp, lb, masks)
        heads = [[q[:, h, :]] for h in range(HEADS)]
        rms(K, "hg_norm", [(x, x, T) for x in heads], P, lambda i, k: K.v("o_norm"))
        with nc.Block() as block:
            @block.vector
            def _(dve):
                for h in range(HEADS):
                    dve.tensor_tensor(q[:, h, :], q[:, h, :], g[:, h, :], ALU.mult)
        residual(K, "hg_out", d["hg_out"], 4, q, KD, 256, LAT, lambda k, s: K.mod[:, 1, k + GATE1, s:s + 1])


def second_block(K):
    modulations(K)
    latent_attention(K)
    feed_forward(K, 0, BOTH)
    gated_recurrence(K)
    feed_forward(K, 1, LAT)


def start(K):
    d = K.dram
    with K.nc.Block() as block:
        here = K.sem("start_here")

        @block.sync
        def _(sp):
            for dst, src in ((K.x[:, :, 0:T], d["x"]), (K.x[:, :, T:N], d["ctx"]), (K.vec[:, :], d["vec"]),
                             (K.ident[:, :], d["ident"])):
                sp.dma_start(dst, src).then_inc(here, 16)
            sp.wait_ge(here, 64)

        @block.vector
        def _(dve):
            dve.memset(K.ones[:, :], 1.0)
            dve.memset(K.eps[:, :], EPS)
    K.end()


def program(nc, dram, out, upto=99, dump=None):
    with ExitStack() as ctx:
        K = Chip(nc, ctx, dram)
        start(K)
        if upto != 2:
            first_block(K)
        if upto != 1:
            second_block(K)
        stored = nc.alloc_semaphore("out_stored")
        with nc.Block() as block:
            @block.sync
            def _(sp):
                sp.dma_start(out, K.x[:, :, 0:T]).then_inc(stored, 16)
                sp.wait_ge(stored, 16)


def panels(w, width):
    kin, kout = w.shape
    return np.ascontiguousarray(
        w.reshape(kin // P, P, kout // width, width).transpose(2, 1, 0, 3).reshape(kout // width, P, -1))


def tokens_last(x):
    t, f = x.shape
    return np.ascontiguousarray(x.T.reshape(f // P, P, t).transpose(1, 0, 2))


def buckets():
    dist = np.maximum(T - 1 - np.arange(SKEW), 0)
    large = 16 + (np.log(np.maximum(dist, 1).astype(np.float32) / 16) / np.float32(np.log(8.0)) * 16).astype(np.int32)
    bucket = np.where(dist < 16, dist, np.minimum(large, 31))
    return (bucket[None, :] == np.arange(32)[:, None]).astype(np.float32)


def rope_tables():
    pos = np.arange(T)
    inv = (10000.0 ** (-np.arange(0, 32, 2, dtype=np.float32) / 32)).astype(np.float32)
    row = (pos // 64).astype(np.float32)[:, None] * inv
    col = (pos % 64).astype(np.float32)[:, None] * inv
    ang = np.concatenate([row, row, col, col], -1)
    rot = np.zeros((64, 64), np.float32)
    for j in range(16):
        rot[16 + j, j], rot[j, 16 + j] = -1, 1
        rot[48 + j, 32 + j], rot[32 + j, 48 + j] = -1, 1
    return np.ascontiguousarray(np.stack([np.cos(ang).T, np.sin(ang).T], 1)).astype(np.float32), rot


def level_masks():
    s, t = np.arange(P)[:, None], np.arange(P)[None, :]
    out = np.zeros((P, 2, LEVELS + 1, P), np.uint32)
    for r in range(2):
        out[:, r, 0] = s == t
        for l in range(LEVELS):
            n = P >> (l + 1)
            parted = (s // (2 * n) == t // (2 * n)) & (s // n != t // n)
            out[:, r, 1 + l] = parted & ((s < t) if r == 0 else (s > t))
    return out


def arrange(a):
    a = {k: np.asarray(v) for k, v in a.items()}
    w_in = a["w_in"][0]
    col = dict(q_a=(0, 512), c_kv=(512, 640), q_idx=(640, 1152), k_idx=(1152, 1216), w_idx=(1216, 1224),
               q_b=(1224, 1736), k_b=(1736, 2248), v_b=(2248, 2760), gate_a=(2760, 3784), gate_b=(3784, 4808))
    part = {k: w_in[:, x:y] for k, (x, y) in col.items()}
    o = {}
    o["x"] = tokens_last(a["x"][0])
    o["ctx"] = tokens_last(a["ctx_2"][0])
    o["p"] = tokens_last(a["p"][0, 0])
    o["w_main"] = panels(np.concatenate([part[k] for k in (
        "q_a", "c_kv", "k_idx", "k_idx", "q_idx", "q_b", "k_b", "gate_a", "gate_b")], 1), 256)
    o["w_vb"] = panels(part["v_b"], 256)
    o["w_idx"] = panels(part["w_idx"], 8)
    o["w_uk"] = np.ascontiguousarray(a["w_uk"][0].transpose(0, 2, 1).reshape(4, 2, HD, P).transpose(1, 2, 0, 3).reshape(P, 4, P))
    o["w_uv"] = np.ascontiguousarray(a["w_uv"][0].transpose(1, 0, 2))
    o["rel_bias"] = a["rel_bias"]
    o["buckets"] = buckets()
    ab = np.stack([a["w_branch_a"][0], a["w_branch_b"][0]]).reshape(2, 4, P, KD, P)
    o["w_branches"] = np.ascontiguousarray(ab.transpose(3, 2, 0, 1, 4).reshape(KD, P, -1))
    o["w_out"] = panels(a["w_out"][0], 256)
    o["w_route"] = np.ascontiguousarray(np.concatenate(
        [a["w_r1"][0], a["w_r2"][0].transpose(1, 0, 2).reshape(D, 32)], 1).reshape(KD, P, 36).transpose(1, 0, 2))
    o["b_route"] = np.concatenate([a["b_r1"][0], a["b_r2"][0].reshape(32)])[None, :]
    for n in ("gate", "up"):
        o[f"w_{n}"] = np.ascontiguousarray(a[f"w_{n}"][0].reshape(N_EXP, KD, P, 256).transpose(0, 2, 1, 3).reshape(N_EXP, P, -1))
    o["w_down"] = np.ascontiguousarray(a["w_down"][0].reshape(N_EXP, 2, P, D).transpose(0, 2, 1, 3).reshape(N_EXP, P, -1))
    ple = np.concatenate([a["w_ple_gate"][0], a["w_ple"][0]], 0)
    o["w_ple"] = panels(ple, P)
    r = np.arange(P)
    o["ident"] = np.eye(P, dtype=np.float32)
    o["masks"] = np.ascontiguousarray(np.stack([
        np.where(r[None, :] <= r[:, None], 0, NEG),
        np.where(r[:, None] < r[None, :], 0, NEG),
        r[:, None] < r[None, :],
        r[:, None] >= r[None, :]], 1).astype(np.float32))
    vecs = dict(attn_norm=a["attn_norm"][0], ffn_norm=a["ffn_norm"][0], ple_norm=a["ple_norm"][0],
                final_norm=a["final_norm"], kv_norm=a["kv_norm"][0],
                norm1_0=a["norm1_w_2"][0], norm1_1=a["norm1_w_2"][1], norm2_0=a["norm2_w_2"][0],
                norm2_1=a["norm2_w_2"][1], q_norm=a["mla_q_norm_w_2"][0], mkv_norm=a["mla_kv_norm_w_2"][0],
                qn=a["mla_qn_w_2"][0], qr=a["mla_qr_w_2"][0], kn=a["mla_kn_w_2"][0], kr=a["mla_kr_w_2"][0],
                o_norm=a["hg_o_norm_w_2"][0], b_ada_0=a["ada_b_2"][0], b_ada_1=a["ada_b_2"][1],
                lb0_f=a["hg_lb_logits_2"][0, 0], lb0_b=a["hg_lb_logits_2"][0, 1],
                lb1_f=a["hg_lb_logits_2"][1, 0], lb1_b=a["hg_lb_logits_2"][1, 1],
                c_lat=a["c_2"][0], c_ctx=a["c_ctx_2"])
    vec = np.zeros((P, VEC_COLS), np.float32)
    for n, (at, cols) in VEC_AT.items():
        v = vecs[n]
        rows = min(P, v.size)
        vec[0:rows, at:at + cols] = v.reshape(cols, rows).T
    o["vec"] = vec
    for i in range(2):
        o[f"ada_{i}"] = panels(a["ada_w_2"][i], 256)
        w13 = np.stack([a["ffn_w1_2"][i].reshape(D, KF, P), a["ffn_w3_2"][i].reshape(D, KF, P)], 2)
        o[f"w13_{i}"] = panels(w13.reshape(D, 2 * D_FF), 256)
        o[f"w2_{i}"] = panels(a["ffn_w2_2"][i], P)
    mla_in = a["mla_w_in_2"][0]
    o["mla_in"] = panels(mla_in[:, :640], P)
    o["mla_in_rope"] = panels(mla_in[:, 640:], 64)
    o["mla_uq"] = panels(a["mla_w_uq_2"][0], 192)
    o["mla_ukv"] = panels(a["mla_w_ukv_2"][0], 256)
    o["mla_out"] = panels(a["mla_w_o_2"][0], 256)
    o["rope"], o["rot"] = rope_tables()
    hg = a["hg_w_in_2"][0]
    part = [hg[:, n * D:(n + 1) * D] for n in range(5)]
    o["hg_in"] = panels(np.concatenate([part[n] for n in (1, 2, 0, 4, 3)], 1), 256)
    o["hg_out"] = panels(a["hg_w_o_2"][0], 256)
    o["levels"] = level_masks()
    return o


OPTIONS = {}


def kernel(**inputs):
    import concourse.bacc as _bacc
    from concourse.bass_utils import run_bass_kernel_spmd as _run

    nc = _bacc.Bacc("TRN2", target_bir_lowering=False, num_devices=1)
    arrays, dram = {}, {}
    for name, a in arrange(inputs).items():
        arrays[f"in_{name}_dram"] = a
        dram[name] = nc.dram_tensor(f"in_{name}_dram", a.shape, mybir.dt.from_np(a.dtype), kind="ExternalInput").ap()
    skew = nc.dram_tensor("bias_skew", (HEADS, P * (SKEW + 1)), F32).ap()
    dram["skew_flat"] = skew
    dram["skew"] = skew.rearrange("h (p n) -> h p n", p=P)
    dram["comb"] = nc.dram_tensor("expert_comb", (N_EXP, T), F32).ap()
    out = nc.dram_tensor("out_0_dram", (P, KD, T), F32, kind="ExternalOutput").ap()
    program(nc, dram, out, **OPTIONS)
    r = _run(nc, [arrays], core_ids=[0])
    got = np.asarray(r.results[0]["out_0_dram"])
    return np.ascontiguousarray(got.transpose(2, 1, 0).reshape(1, T, D))
```

```python
from contextlib import ExitStack

import numpy as np

import concourse.bass as bass
from concourse import mybir

F32 = mybir.dt.float32
F32R = mybir.dt.float32r
U32 = mybir.dt.uint32
ALU = mybir.AluOpType
ACT = mybir.ActivationFunctionType
AX = mybir.AxisListType.X
ds = bass.ds

P = 128
D = 1024
KD = D // P
T = 512
C = 256
N = T + C
QT = T // P
EPS = 1e-6
HEADS = 8
HD = 64
TOPK = 128
NEG = -1e30
TAKEN = -3e38
N_EXP = 32
D_FF = 2816
KF = D_FF // P
RING = 4
PAIR = 2
BANK = 512
LOG_EXP = "natural_log_exp_and_others"


def each_round(eng, panels, ring, body):
    full, rest = divmod(panels, ring)
    if full > 1:
        with eng.Fori(0, full) as i:
            body(i, ring)
    elif full == 1:
        body(0, ring)
    if rest:
        body(full, rest)


def each_ahead(eng, panels, ring, early, late):
    full, rest = divmod(panels - 1, ring)
    early(0, 0)
    if full > 1:
        with eng.Fori(0, full) as i:
            for j in range(ring):
                early(i + (j + 1) // ring, (j + 1) % ring)
                late(i, j)
    elif full:
        for j in range(ring):
            early((j + 1) // ring, (j + 1) % ring)
            late(0, j)
    for j in range(rest):
        early(full + (j + 1) // ring, (j + 1) % ring)
        late(full, j)
    late((panels - 1) // ring, (panels - 1) % ring)


class Two:

    def __init__(self, high, low):
        self.high, self.low = high, low

    def __getitem__(self, at):
        return Two(self.high[at], self.low[at])


def multiply(pe, out, lhs, rhs, start, stop):
    if not isinstance(lhs, Two):
        return pe.matmul(out, lhs, rhs, start=start, stop=stop)
    pe.matmul(out, lhs.high, rhs.high, start=start, stop=False)
    pe.matmul(out, lhs.high, rhs.low, start=False, stop=False)
    return pe.matmul(out, lhs.low, rhs.high, start=False, stop=stop)


class Chip:

    def __init__(self, nc, ctx, dram):
        self.nc, self.ctx, self.dram, self.own = nc, ctx, dram, []
        self.x = self.sb("residual", [P, KD, N])
        self.ones = self.sb("ones", [P, P])
        self.ident = self.sb("ident", [P, P])
        self.eps = self.sb("eps", [P, 1])
        self.vec = self.sb("vectors", [P, VEC_COLS])
        self.mod = self.sb("modulation", [P, 2, 48, 2])
        self.gain = self.sb("gains", [P, 2, 2, KD, 2])
        self.ps = ctx.enter_context(nc.psum_tensor("ps", [P, 8, BANK], F32))
        self.psf = self.ps[:, :, :].rearrange("p b n -> p (b n)")

    def sb(self, name, shape, dt=F32):
        return self.ctx.enter_context(self.nc.sbuf_tensor(name, shape, dt))

    def sem(self, name):
        s = self.nc.alloc_semaphore(name)
        self.own.append(s)
        return s

    def two(self, own, name, shape):
        t = own.enter_context(self.nc.sbuf_tensor(name, [P, 2] + shape, F32R))
        return Two(t[:, 0], t[:, 1])

    def scratch(self, own, name, words):
        self.flat = own.enter_context(self.nc.sbuf_tensor(name, [P, words], F32))[:, :]

    def end(self):
        for s in self.own:
            self.nc.gpsimd.sem_clear(s)
            self.nc.release_semaphore(s)
        self.own = []

    def v(self, name, k=0, rows=P):
        at = VEC_AT[name][0] + k
        return self.vec[0:rows, at:at + 1]


VECS = [("attn_norm", KD), ("ffn_norm", KD), ("ple_norm", KD), ("final_norm", KD), ("kv_norm", 1),
        ("norm1_0", KD), ("norm1_1", KD), ("norm2_0", KD), ("norm2_1", KD),
        ("q_norm", 3), ("mkv_norm", 2), ("qn", 1), ("qr", 1), ("kn", 1), ("kr", 1),
        ("o_norm", 1), ("b_ada_0", 48), ("b_ada_1", 48), ("lb0_f", KD), ("lb0_b", KD),
        ("lb1_f", KD), ("lb1_b", KD), ("c_lat", KD), ("c_ctx", KD)]
VEC_AT = {}
VEC_COLS = 0
for _name, _n in VECS:
    VEC_AT[_name] = (VEC_COLS, _n)
    VEC_COLS += _n


def linear(K, name, w, panels, banks, groups, words, on_act=None, on_dve=None, first=0, split=True):
    nc = K.nc
    ring = PAIR if split else RING
    turns = min(ring, 8 // banks)
    loaded = [K.sem(f"{name}_loaded{j}") for j in range(ring)]
    raised = [K.sem(f"{name}_raised{j}") for j in range(ring)]
    lowered = [K.sem(f"{name}_lowered{j}") for j in range(ring)]
    product = [K.sem(f"{name}_product{j}") for j in range(ring)]
    act_done = [K.sem(f"{name}_act{j}") for j in range(ring)] if on_act else None
    dve_done = [K.sem(f"{name}_dve{j}") for j in range(ring)] if on_dve else None

    def set_of(j):
        t = j % turns
        return [K.ps[:, b, :] for b in range(t * banks, (t + 1) * banks)]

    with ExitStack() as own:
        raw = own.enter_context(nc.sbuf_tensor(f"{name}_raw", [P, ring, words], F32))
        parts = K.two(own, f"{name}_split", [ring, words]) if split else None
        block = own.enter_context(nc.Block())

        @block.sync
        def _(sp):
            def body(i, n):
                for j in range(n):
                    sp.wait_ge((lowered if split else product)[j], i + 1)
                    sp.dma_start(raw[:, j, :], w[first + i * ring + j]).then_inc(loaded[j], 16)
            each_round(sp, panels, ring, body)

        if split:
            @block.gpsimd
            def _(pool):
                def body(i, n):
                    for j in range(n):
                        pool.wait_ge(raised[j], i + 1)
                        pool.tensor_tensor(parts.low[:, j, :], raw[:, j, :], parts.high[:, j, :].bitcast(F32),
                                           ALU.subtract).then_inc(lowered[j], 1)
                for j in range(ring):
                    pool.sem_inc(lowered[j], 1)
                each_round(pool, panels, ring, body)

        @block.tensor
        def _(pe):
            def body(i, n):
                for j in range(n):
                    for done in (act_done, dve_done):
                        if done and j < turns:
                            pe.wait_ge(done[max(s for s in range(ring) if s % turns == j)], i + 1)
                        elif done:
                            pe.wait_ge(done[j - turns], i + 2)
                    if split:
                        pe.wait_ge(lowered[j], i + 2)
                    else:
                        pe.wait_ge(loaded[j], (i + 1) * 16)
                    slot = parts[:, j, :] if split else raw[:, j, :]
                    for b, at, cols, rows, terms in groups(slot):
                        for t, (lhs, rhs) in enumerate(terms):
                            mm = multiply(pe, set_of(j)[b][0:rows, at:at + cols], lhs, rhs, t == 0,
                                          t == len(terms) - 1)
                    mm.then_inc(product[j], 1)
            for j in range(ring):
                pe.sem_inc(product[j], 1)
            each_round(pe, panels, ring, body)

        if split or on_act:
            @block.scalar
            def _(act):
                def raise_(i, j):
                    act.wait_ge(loaded[j], (i + 1) * 16)
                    act.wait_ge(product[j], i + 1)
                    act.activation(parts.high[:, j, :], raw[:, j, :], ACT.Copy).then_inc(raised[j], 1)

                def take(i, j):
                    act.wait_ge(product[j], i + 2)
                    on_act(act, i * ring + j, set_of(j), j).then_inc(act_done[j], 1)

                if on_act:
                    for j in range(ring):
                        act.sem_inc(act_done[j], 1)
                if split and on_act:
                    each_ahead(act, panels, ring, raise_, take)
                else:
                    def body(i, n):
                        for j in range(n):
                            (raise_ if split else take)(i, j)
                    each_round(act, panels, ring, body)

        if on_dve:
            @block.vector
            def _(dve):
                def body(i, n):
                    for j in range(n):
                        dve.wait_ge(product[j], i + 2)
                        if act_done:
                            dve.wait_ge(act_done[j], i + 2)
                        on_dve(dve, i * ring + j, set_of(j), j).then_inc(dve_done[j], 1)
                for j in range(ring):
                    dve.sem_inc(dve_done[j], 1)
                each_round(dve, panels, ring, body)
    K.end()


def features_out(acts, kc, width, spans):
    def groups(slot):
        out = []
        for w in range(width // P):
            for s, (a, c) in enumerate(spans):
                out.append((w * len(spans) + s, 0, c, P,
                            [(slot[:, k * width + w * P:k * width + (w + 1) * P], acts[:, k, a:a + c])
                             for k in range(kc)]))
        return out
    return groups


def split(K, name, pairs):
    nc = K.nc
    raised = K.sem(f"{name}_raised")
    with nc.Block() as block:
        @block.scalar
        def _(act):
            for src, dst in pairs:
                act.activation(dst.high, src, ACT.Copy).then_inc(raised, 1)

        @block.vector
        def _(dve):
            for n, (src, dst) in enumerate(pairs):
                if n % 3 < 2:
                    dve.wait_ge(raised, n + 1)
                    dve.tensor_tensor(dst.low, src, dst.high.bitcast(F32), ALU.subtract)

        @block.gpsimd
        def _(pool):
            for n, (src, dst) in enumerate(pairs):
                if n % 3 == 2:
                    pool.wait_ge(raised, n + 1)
                    pool.tensor_tensor(dst.low, src, dst.high.bitcast(F32), ALU.subtract)
    K.end()


def load(K, name, pairs):
    with K.nc.Block() as block:
        here = K.sem(f"{name}_here")

        @block.sync
        def _(sp):
            for dst, src in pairs:
                sp.dma_start(dst, src).then_inc(here, 16)
            sp.wait_ge(here, 16 * len(pairs))
    K.end()


def rms(K, name, items, width, gain, shift=None, rows=P, parts=None):
    nc = K.nc
    squared, summed = K.sem(f"{name}_squared"), K.sem(f"{name}_summed")
    rooted, scaled = K.sem(f"{name}_rooted"), K.sem(f"{name}_scaled")
    inverted, raised = K.sem(f"{name}_inverted"), K.sem(f"{name}_raised")
    with ExitStack() as own:
        sqs = own.enter_context(nc.sbuf_tensor(f"{name}_sq", [P, 2, BANK], F32))
        root = own.enter_context(nc.sbuf_tensor(f"{name}_root", [P, 2, BANK], F32))
        inv = own.enter_context(nc.sbuf_tensor(f"{name}_inv", [P, 2, BANK], F32))
        steps = [(i, k) for i, (src, _, _) in enumerate(items) for k in range(len(src))]
        upto = [0]
        for src, _, _ in items:
            upto.append(upto[-1] + len(src))
        block = own.enter_context(nc.Block())

        @block.scalar
        def _(act):
            def root_of(i):
                c = items[i][2]
                act.wait_ge(summed, upto[i + 1])
                if i >= 2:
                    act.wait_ge(inverted, i - 1)
                act.activation(root[0:rows, i % 2, 0:c], K.ps[0:rows, i % 4, 0:c], ACT.Sqrt,
                               scale=1.0 / width, bias=K.eps[0:rows, :]).then_inc(rooted, 1)
            for n, (i, k) in enumerate(steps):
                if k == 0 and i > 0:
                    root_of(i - 1)
                if n >= 2:
                    act.wait_ge(summed, n - 1)
                act.activation(sqs[0:rows, n % 2, 0:items[i][2]], items[i][0][k], ACT.Square).then_inc(squared, 1)
            root_of(len(items) - 1)
            if parts:
                for n, (i, k) in enumerate(steps):
                    act.wait_ge(scaled, n + 1)
                    act.activation(parts[i][k].high, items[i][1][k], ACT.Identity,
                                   bias=shift(i, k) if shift else 0.0).then_inc(raised, 1)

        @block.tensor
        def _(pe):
            for n, (i, k) in enumerate(steps):
                c = items[i][2]
                if k == 0 and i >= 4:
                    pe.wait_ge(rooted, i - 3)
                pe.wait_ge(squared, n + 1)
                pe.matmul(K.ps[0:rows, i % 4, 0:c], K.ones[0:rows, 0:rows], sqs[0:rows, n % 2, 0:c],
                          start=k == 0, stop=n + 1 == upto[i + 1]).then_inc(summed, 1)

        @block.vector
        def _(dve):
            for i, (src, dst, c) in enumerate(items):
                dve.wait_ge(rooted, i + 1)
                if i >= 2:
                    dve.wait_ge(scaled, upto[i - 1])
                dve.reciprocal(inv[0:rows, i % 2, 0:c], root[0:rows, i % 2, 0:c]).then_inc(inverted, 1)
                dve.wait_ge(inverted, i + 1)
                for k in range(len(src)):
                    dve.scalar_tensor_tensor(out=dst[k], in0=src[k], scalar=gain(i, k), in1=inv[0:rows, i % 2, 0:c],
                                             op0=ALU.mult, op1=ALU.mult).then_inc(scaled, 1)
            if parts:
                for n, (i, k) in enumerate(steps):
                    dve.wait_ge(raised, n + 1)
                    dve.scalar_tensor_tensor(out=parts[i][k].low, in0=items[i][1][k],
                                             scalar=shift(i, k) if shift else 0.0,
                                             in1=parts[i][k].high.bitcast(F32), op0=ALU.add, op1=ALU.subtract)
    K.end()


def norm_model(K, own, name, spans, gain, shift=None, room=None):
    h = K.two(own, f"{name}_h", [KD, sum(c for _, c in spans)])
    with ExitStack() as here:
        y = room or here.enter_context(K.nc.sbuf_tensor(f"{name}_y", [P, KD, N], F32))
        items = [([K.x[:, k, a:a + c] for k in range(KD)], [y[:, k, a:a + c] for k in range(KD)], c)
                 for a, c in spans]
        rms(K, name, items, D, gain, shift, parts=[[h[:, k, a:a + c] for k in range(KD)] for a, c in spans])
    return h


LAT = [(0, T)]
BOTH = [(0, T), (T, C)]

QA, CKV, KIDX, QIDX, QB, KB = 0, 4, 5, 6, 10, 14


def copy_pair(dst):
    def take(dve, m, banks, j):
        dve.tensor_copy(dst[:, m * 2, :], banks[0])
        return dve.tensor_copy(dst[:, m * 2 + 1, :], banks[1])
    return take


def activate_pair(dst, func):
    def take(act, m, banks, j):
        act.activation(dst[:, m * 2, :], banks[0], func)
        return act.activation(dst[:, m * 2 + 1, :], banks[1], func)
    return take


def tokens_out(acts, tiles, width):
    per = BANK // width
    return lambda slot: [(t // per, (t % per) * width, width, P,
                          [(acts[:, k, t * P:(t + 1) * P], slot[:, k * width:(k + 1) * width]) for k in range(KD)])
                         for t in range(tiles)]


def project_in(K, h, proj, gates, vb, widx):
    groups = features_out(h, KD, 256, LAT)
    linear(K, "w_in", K.dram["w_main"], 9, 2, groups, 2048, on_dve=copy_pair(proj))
    linear(K, "w_gates", K.dram["w_main"], 8, 2, groups, 2048, on_act=activate_pair(gates, ACT.Sigmoid), first=9)

    def take_v(dve, m, banks, j):
        for q in range(QT):
            last = dve.tensor_copy(vb[:, q, ds(m * 256, 256)], banks[q // 2][:, (q % 2) * 256:(q % 2 + 1) * 256])
        return last
    linear(K, "w_vb", K.dram["w_vb"], 2, 2, tokens_out(h, QT, 256), 2048, on_dve=take_v)

    def take_w(dve, m, banks, j):
        return dve.tensor_scalar(widx[:, :], banks[0][:, 0:QT * 8], (HEADS ** -0.5) * (HD ** -0.5), None, ALU.mult)
    linear(K, "w_idx", K.dram["w_idx"], 1, 2, tokens_out(h, QT, 8), 64, on_dve=take_w)


def bias_tiles(K):
    nc, d = K.nc, K.dram
    made, taken, stored, back, here = (K.sem(f"bias_{n}") for n in ("made", "taken", "stored", "back", "here"))
    with ExitStack() as own:
        rel = own.enter_context(nc.sbuf_tensor("rel", [32, HEADS], F32))
        wide = own.enter_context(nc.sbuf_tensor("rel_wide", [32, HEADS, P], F32))
        hot = own.enter_context(nc.sbuf_tensor("bucket_hot", [32, SKEW], F32))
        rows = K.flat[:, 0:HEADS * SKEW].rearrange("p (h n) -> p h n", h=HEADS)
        spread = K.sem("bias_spread")
        block = own.enter_context(nc.Block())

        @block.sync
        def _(sp):
            sp.dma_start(rel[:, :], d["rel_bias"]).then_inc(here, 16)
            sp.dma_start(hot[:, :], d["buckets"]).then_inc(here, 16)
            sp.wait_ge(taken, 2 * HEADS)
            sp.dma_start(d["skew"][:, :, 0:SKEW].rearrange("h p n -> p h n"), rows).then_inc(stored, 16)
            sp.wait_ge(stored, 16)
            skewed = d["skew_flat"][:, 0:P * SKEW].rearrange("h (p n) -> p h n", p=P)
            sp.dma_start(K.bias, skewed[:, :, P - 1:P - 1 + T]).then_inc(back, 16)
            sp.wait_ge(back, 16)

        @block.vector
        def _(dve):
            dve.wait_ge(here, 32)
            dve.tensor_copy(wide[:, :, :], rel[:, :].unsqueeze(2).to_broadcast([32, HEADS, P])).then_inc(spread, 1)
            for n in range(2 * HEADS):
                h, half = divmod(n, 2)
                dve.wait_ge(made, n + 1)
                dve.tensor_copy(rows[:, h, half * SKEW // 2:(half + 1) * SKEW // 2],
                                K.ps[:, n % 4, 0:SKEW // 2]).then_inc(taken, 1)

        @block.tensor
        def _(pe):
            pe.wait_ge(spread, 1)
            for n in range(2 * HEADS):
                h, half = divmod(n, 2)
                if n >= 4:
                    pe.wait_ge(taken, n - 3)
                pe.matmul(K.ps[:, n % 4, 0:SKEW // 2], wide[:, h, :], hot[:, half * SKEW // 2:(half + 1) * SKEW // 2],
                          start=True, stop=True).then_inc(made, 1)
    K.end()


SKEW = 640


def half(h):
    return (h % 2) * HD, (h % 2 + 1) * HD


def select_keys(K, proj, widx, maskadd, cneg):
    nc = K.nc
    scored, positive, summed, chain = (K.sem(f"sel_{n}") for n in ("scored", "positive", "summed", "chain"))
    rel = K.flat[:, 0:2 * T].rearrange("p (b n) -> p b n", b=2)
    score = K.flat[:, 2 * T:4 * T].rearrange("p (b n) -> p b n", b=2)
    top = K.flat[:, 4 * T:4 * T + 8]
    tasks = [(i, h) for i in range(1, QT) for h in range(HEADS)]
    with nc.Block() as block:
        @block.tensor
        def _(pe):
            for n, (i, h) in enumerate(tasks):
                a, b = half(h)
                if n >= 4:
                    pe.wait_ge(positive, n - 3)
                pe.matmul(K.ps[:, n % 4, 0:(i + 1) * P], proj[a:b, QIDX + h // 2, i * P:(i + 1) * P],
                          proj[a:b, KIDX, 0:(i + 1) * P], start=True, stop=True).then_inc(scored, 1)

        @block.scalar
        def _(act):
            for n, (i, h) in enumerate(tasks):
                act.wait_ge(scored, n + 1)
                if n >= 2:
                    act.wait_ge(summed, n - 1)
                act.activation(rel[:, n % 2, 0:(i + 1) * P], K.ps[:, n % 4, 0:(i + 1) * P],
                               ACT.Relu).then_inc(positive, 1)

        @block.vector
        def _(dve):
            steps = [0]

            def link(ins):
                steps[0] += 1
                ins.then_inc(chain, 1)
                dve.wait_ge(chain, steps[0])

            dve.tensor_copy(maskadd[:, 0, 0:P], cneg)
            for n, (i, h) in enumerate(tasks):
                w = (i + 1) * P
                s = score[:, i % 2, 0:w]
                dve.wait_ge(positive, n + 1)
                if h == 0:
                    dve.tensor_scalar(s, rel[:, n % 2, 0:w], widx[:, i * 8 + h:i * 8 + h + 1], None,
                                      ALU.mult).then_inc(summed, 1)
                else:
                    dve.scalar_tensor_tensor(out=s, in0=rel[:, n % 2, 0:w], scalar=widx[:, i * 8 + h:i * 8 + h + 1],
                                             in1=s, op0=ALU.mult, op1=ALU.add).then_inc(summed, 1)
                dve.wait_ge(summed, n + 1)
                if h == HEADS - 1:
                    diag = score[:, i % 2, i * P:w]
                    link(dve.tensor_tensor(diag, diag, cneg, ALU.add))
                    for _ in range(TOPK // 8):
                        link(dve.max(top, s))
                        link(dve.match_replace(s, top, s, TAKEN))
                    dve.tensor_scalar(maskadd[:, i, 0:w], s, TAKEN / 2, NEG, ALU.is_gt, ALU.mult)
    K.end()


def attend(K, name, tasks, spare, heads, scale, values, out, bias=False):
    nc = K.nc
    names = ("scored", "shown", "maxed", "exped", "normed", "turned", "copied", "valued", "outed", "chain")
    scored, shown, maxed, exped, normed, turned, copied, valued, outed, chain = (
        K.sem(f"{name}_{n}") for n in names)
    blocks, queries, width = spare
    at = [0]

    def part(*shape):
        n = int(np.prod(shape))
        ap = K.flat[:, at[0]:at[0] + n]
        at[0] += n
        return ap

    turn = [part(blocks * queries).rearrange("p (k q) -> p k q", k=blocks) for _ in range(2)]
    prob = [part(width) for _ in range(2)]
    logit = [part(width) for _ in range(2)] if bias else None
    last = [t + 1 == len(tasks) or tasks[t + 1][0] != task[0] for t, task in enumerate(tasks)]
    outs = len(out(0))
    with ExitStack() as own:
        small = own.enter_context(nc.sbuf_tensor(f"{name}_small", [P, 4, 4], F32))
        block = own.enter_context(nc.Block())

        def raw(n):
            b = (n % 2) * 2 * BANK
            return K.psf[:, b:b + tasks[n][1]]

        @block.tensor
        def _(pe):
            def scores(n):
                _, w, terms, _, _, _, _ = tasks[n]
                if n >= 2:
                    pe.wait_ge(shown if bias else exped, n - 1)
                    pe.wait_ge(exped, n - 1)
                for c in range(0, w, BANK):
                    e = min(w, c + BANK)
                    for t, (q, k) in enumerate(terms):
                        mm = pe.matmul(raw(n)[:, c:e], q, k[:, c:e], start=t == 0, stop=t == len(terms) - 1)
                mm.then_inc(scored, 1)

            scores(0)
            for n, (h, w, _, _, _, _, _) in enumerate(tasks):
                if n + 1 < len(tasks):
                    scores(n + 1)
                pe.wait_ge(normed, n + 1)
                if n >= 1:
                    pe.wait_ge(copied, n)
                for b in range(w // P):
                    mm = pe.transpose(K.psf[:, 4 * BANK + b * P:4 * BANK + (b + 1) * P],
                                      prob[n % 2][:, b * P:(b + 1) * P], K.ident[:, :])
                mm.then_inc(turned, 1)
                if last[n]:
                    pe.wait_ge(copied, n + 1)
                    if h >= 1:
                        pe.wait_ge(outed, h)
                    for bank, a, e, terms in values(h, turn[h % 2]):
                        for t, (v, p, x) in enumerate(terms):
                            mm = pe.matmul(K.ps[:, bank, a + x:e], v, p, start=t == 0, stop=t == len(terms) - 1)
                    mm.then_inc(valued, 1)

        @block.vector
        def _(dve):
            links = [0]

            def link(ins):
                links[0] += 1
                ins.then_inc(chain, 1)
                dve.wait_ge(chain, links[0])

            def top(n):
                w = tasks[n][1]
                dve.wait_ge(scored, n + 1)
                if n >= 4:
                    dve.wait_ge(exped, n - 3)
                s = raw(n)
                if bias:
                    s = logit[n % 2][:, 0:w]
                    if n >= 2:
                        dve.wait_ge(exped, n - 1)
                    dve.scalar_tensor_tensor(out=s, in0=raw(n), scalar=scale, in1=tasks[n][5],
                                             op0=ALU.mult, op1=ALU.add).then_inc(shown, 1)
                    dve.wait_ge(shown, n + 1)
                    link(dve.tensor_tensor(s, s, tasks[n][6], ALU.add))
                link(dve.reduce_max(small[:, n % 4, 0:1], s, AX))
                dve.tensor_scalar(small[:, n % 4, 1:2], small[:, n % 4, 0:1], -1.0 if bias else -scale, None,
                                  ALU.mult).then_inc(maxed, 1)

            def outputs(dve, h):
                dve.wait_ge(valued, h + 1)
                for dst, bank, c in out(h):
                    ins = dve.tensor_copy(dst, K.ps[:, bank, 0:c])
                ins.then_inc(outed, 1)

            top(0)
            for n, (h, w, _, _, _, _, _) in enumerate(tasks):
                if n + 1 < len(tasks):
                    top(n + 1)
                dve.wait_ge(exped, n + 1)
                link(dve.reciprocal(small[:, n % 4, 3:4], small[:, n % 4, 2:3]))
                dve.tensor_scalar(prob[n % 2][:, 0:w], prob[n % 2][:, 0:w], small[:, n % 4, 3:4], None,
                                  ALU.mult).then_inc(normed, 1)
                if last[n] and h >= 1:
                    outputs(dve, h - 1)
            outputs(dve, heads - 1)

        @block.scalar
        def _(act):
            def exp(n):
                w = tasks[n][1]
                act.wait_ge(maxed, n + 1)
                if n >= 2:
                    act.wait_ge(turned, n - 1)
                act.activation(prob[n % 2][:, 0:w], logit[n % 2][:, 0:w] if bias else raw(n), ACT.Exp,
                               bias=small[:, n % 4, 1:2], scale=1.0 if bias else scale,
                               accum_out=small[:, n % 4, 2:3]).then_inc(exped, 1)

            exp(0)
            for n, (h, w, _, k0, q0, _, _) in enumerate(tasks):
                if n + 1 < len(tasks):
                    exp(n + 1)
                act.wait_ge(turned, n + 1)
                if h >= 2:
                    act.wait_ge(valued, h - 1)
                act.activation(turn[h % 2][:, k0:k0 + w // P, q0:q0 + P],
                               K.psf[:, 4 * BANK:4 * BANK + w].rearrange("p (k q) -> p k q", q=P),
                               ACT.Copy).then_inc(copied, 1)
    K.end()


def products(K, name, items):
    nc = K.nc
    made, taken = K.sem(f"{name}_made"), K.sem(f"{name}_taken")
    with nc.Block() as block:
        @block.tensor
        def _(pe):
            for n, ((a, b), cols, terms, _) in enumerate(items):
                if n >= 8:
                    pe.wait_ge(taken, n - 7)
                for t, (lhs, rhs) in enumerate(terms):
                    mm = pe.matmul(K.ps[a:b, n % 8, 0:cols], lhs, rhs, start=t == 0, stop=t == len(terms) - 1)
                mm.then_inc(made, 1)

        @block.vector
        def _(dve):
            for n, ((a, b), cols, _, dst) in enumerate(items):
                dve.wait_ge(made, n + 1)
                dve.tensor_copy(dst, K.ps[a:b, n % 8, 0:cols]).then_inc(taken, 1)
    K.end()


def sparse_attention(K, proj, widx, cneg, heads_out):
    nc, d = K.nc, K.dram
    with ExitStack() as own:
        maskadd = own.enter_context(nc.sbuf_tensor("maskadd", [P, QT, T], F32))
        c_nat = own.enter_context(nc.sbuf_tensor("c_nat", [P, QT, P], F32))
        w_uk = own.enter_context(nc.sbuf_tensor("w_uk", [P, HEADS // 2, P], F32))
        w_uv = own.enter_context(nc.sbuf_tensor("w_uv", [P, HEADS, HD], F32))
        load(K, "load_uk", [(w_uk[:, :, :], d["w_uk"]), (w_uv[:, :, :], d["w_uv"])])
        rms(K, "kv_norm", [([proj[:, CKV, :]], [proj[:, CKV, :]], T)], P, lambda i, k: K.v("kv_norm"))
        select_keys(K, proj, widx, maskadd, cneg)
        bias_tiles(K)
        items = [((0, P), P, [(proj[:, CKV, q * P:(q + 1) * P], K.ident[:, :])], c_nat[:, q, :]) for q in range(QT)]
        q_abs = heads_out
        for h in range(HEADS):
            a, b = half(h)
            items.append(((0, P), T, [(w_uk[a:b, h // 2, :], proj[a:b, QA + h // 2, :])], q_abs[:, h, 0:T]))
        products(K, "q_abs", items)

        def o_at(h):
            return proj[:, QA + h if h < 4 else QIDX + h - 4, :]

        tasks = []
        for h in range(HEADS):
            for i in range(QT):
                w = (i + 1) * P
                tasks.append((h, w, [(q_abs[:, h, i * P:w], proj[:, CKV, 0:w])], 0, i * P,
                              K.bias[:, h, T - w:T], maskadd[:, i, 0:w]))

        def values(h, turn):
            return [(6, 0, T, [(c_nat[:, b, :], turn[:, b, b * P:T], b * P) for b in range(QT)])]
        attend(K, "dsa", tasks, (QT, T, T), HEADS, HD ** -0.5, values, lambda h: [(o_at(h), 6, T)], bias=True)
        products(K, "w_uv", [(half(h), T, [(w_uv[:, h, :], o_at(h))], heads_out[half(h)[0]:half(h)[1], h // 2, 0:T])
                             for h in range(HEADS)])


def stick_breaking(K, proj, vb, sneg, s01, upper, heads_out):
    nc = K.nc
    names = ("scored", "scaled", "folded", "faded", "softened", "masked", "summed", "logged", "weighed", "valued", "outed")
    scored, scaled, folded, faded, softened, masked, summed, logged, weighed, valued, outed = (
        K.sem(f"stick_{n}") for n in names)
    tasks = [(h, b) for h in range(HEADS) for b in reversed(range(QT))]
    z = K.flat[:, 0:2 * QT * T].rearrange("p (u b q) -> p u b q", u=2, b=QT)
    sp = K.flat[:, 2 * QT * T:4 * QT * T].rearrange("p (u b q) -> p u b q", u=2, b=QT)
    tmp = K.flat[:, 4 * QT * T:4 * QT * T + 4 * T].rearrange("p (u q) -> p u q", u=4)
    with nc.Block() as block:
        @block.tensor
        def _(pe):
            def scores(n):
                h, b = tasks[n]
                a, e = half(h)
                if n >= 3:
                    pe.wait_ge(scaled, n - 2)
                pe.matmul(K.ps[:, n % 3, b * P:T], proj[a:e, KB + h // 2, b * P:(b + 1) * P],
                          proj[a:e, QB + h // 2, b * P:T], start=True, stop=True).then_inc(scored, 1)

            def sums(n):
                h, b = tasks[n]
                pe.wait_ge(masked, n + 1)
                if n >= 3:
                    pe.wait_ge(logged, n - 2)
                for c in range(b, QT):
                    mm = pe.matmul(K.ps[:, 3 + n % 3, c * P:T], upper if c == b else K.ones[:, :],
                                   sp[:, h % 2, c, c * P:T], start=c == b, stop=c == QT - 1)
                mm.then_inc(summed, 1)

            def value(h):
                a, e = half(h)
                pe.wait_ge(weighed, QT * (h + 1))
                if h >= 2:
                    pe.wait_ge(outed, h - 1)
                for b in range(QT):
                    mm = pe.matmul(K.ps[a:e, 6 + h % 2, b * P:T], vb[:, b, h * HD:(h + 1) * HD],
                                   z[:, h % 2, b, b * P:T], start=b == 0, stop=b == QT - 1)
                mm.then_inc(valued, 1)

            for n in range(2):
                scores(n)
            for n, (h, b) in enumerate(tasks):
                if n + 2 < len(tasks):
                    scores(n + 2)
                sums(n)
                if b == 2 and h >= 1:
                    value(h - 1)
            value(HEADS - 1)

        @block.scalar
        def _(act):
            def soften(n):
                h, b = tasks[n]
                t = tmp[:, n % 4, b * P:T]
                act.wait_ge(scored, n + 1)
                if h >= 2:
                    act.wait_ge(valued, h - 1)
                act.activation(z[:, h % 2, b, b * P:T], K.ps[:, n % 3, b * P:T], ACT.Copy,
                               scale=HD ** -0.5).then_inc(scaled, 1)
                if n >= 4:
                    act.wait_ge(masked, n - 3)
                act.wait_ge(scaled, n + 1)
                act.activation(t, z[:, h % 2, b, b * P:T], ACT.Abs).then_inc(folded, 1)
                act.wait_ge(folded, n + 1)
                act.activation(t, t, ACT.Exp, scale=-1.0).then_inc(faded, 1)
                act.wait_ge(faded, n + 1)
                act.activation(t, t, ACT.Ln, bias=1.0).then_inc(softened, 1)

            def weigh(n):
                h, b = tasks[n]
                act.wait_ge(logged, n + 1)
                act.activation(z[:, h % 2, b, b * P:T], z[:, h % 2, b, b * P:T], ACT.Exp).then_inc(weighed, 1)

            act.preload_act_table_set(LOG_EXP)
            soften(0)
            for n in range(len(tasks)):
                if n + 1 < len(tasks):
                    soften(n + 1)
                weigh(n)

        @block.vector
        def _(dve):
            steps = [0]
            chain = K.sem("stick_chain")

            def link(ins):
                steps[0] += 1
                ins.then_inc(chain, 1)
                dve.wait_ge(chain, steps[0])

            def plus(n):
                h, b = tasks[n]
                dve.wait_ge(softened, n + 1)
                if h >= 2:
                    dve.wait_ge(summed, QT * (h - 1))
                s, diag = sp[:, h % 2, b, b * P:T], sp[:, h % 2, b, b * P:(b + 1) * P]
                link(dve.scalar_tensor_tensor(out=s, in0=z[:, h % 2, b, b * P:T], scalar=0.0,
                                              in1=tmp[:, n % 4, b * P:T], op0=ALU.max, op1=ALU.add))
                dve.tensor_tensor(diag, diag, s01, ALU.mult).then_inc(masked, 1)

            def out(dve, h):
                a, e = half(h)
                dve.wait_ge(valued, h + 1)
                dve.tensor_copy(heads_out[a:e, 4 + h // 2, 0:T], K.ps[a:e, 6 + h % 2, :]).then_inc(outed, 1)

            plus(0)
            for n, (h, b) in enumerate(tasks):
                if n + 1 < len(tasks):
                    plus(n + 1)
                dve.wait_ge(summed, n + 1)
                zz, diag = z[:, h % 2, b, b * P:T], z[:, h % 2, b, b * P:(b + 1) * P]
                link(dve.tensor_tensor(zz, zz, K.ps[:, 3 + n % 3, b * P:T], ALU.subtract))
                dve.tensor_tensor(diag, diag, sneg, ALU.add).then_inc(logged, 1)
                if b == 0 and h >= 1:
                    out(dve, h - 1)
            out(dve, HEADS - 1)

    K.end()


def merge(K, heads_out, gates):
    d = K.dram
    with ExitStack() as own:
        merged = own.enter_context(K.nc.sbuf_tensor("merged", [P, KD, T], F32))
        with ExitStack() as here:
            o = K.two(here, "heads_out_parts", [KD, T])
            split(K, "split_heads", [(heads_out[:, k, :], o[:, k, :]) for k in range(KD)])

            def groups(slot):
                return [(s, 0, T, P, [(slot[:, (s * 4 + k) * P:(s * 4 + k + 1) * P], o[:, s * 4 + k, :])
                                      for k in range(4)]) for s in range(2)]
            gated = here.enter_context(K.nc.sbuf_tensor("gated", [P, PAIR, 2, T], F32))
            both = K.sem("merge_both")

            def take(dve, m, banks, j):
                dve.tensor_tensor(gated[:, j, 0, :], banks[0], gates[:, m, :], ALU.mult)
                dve.tensor_tensor(gated[:, j, 1, :], banks[1], gates[:, KD + m, :], ALU.mult).then_inc(both, 1)
                dve.wait_ge(both, m + 1)
                return dve.tensor_tensor(merged[:, m, :], gated[:, j, 0, :], gated[:, j, 1, :], ALU.add)
            linear(K, "branches", d["w_branches"], KD, 2, groups, 1024, on_dve=take)
        residual_of(K, "w_out", d["w_out"], 4, merged, KD, 256, LAT)


def residual_of(K, name, w, panels, acts, kc, width, spans, gate=None):
    with ExitStack() as own:
        parts = K.two(own, f"{name}_acts", [kc, sum(c for _, c in spans)])
        split(K, f"{name}_split", [(acts[:, k, :], parts[:, k, :]) for k in range(kc)])
        residual(K, name, w, panels, parts, kc, width, spans, gate)


def residual(K, name, w, panels, acts, kc, width, spans, gate=None, first=0):
    per = width // P
    n = len(spans)

    def take(dve, m, banks, j):
        for u in range(per):
            for s, (a, c) in enumerate(spans):
                x = K.x[:, m * per + u, a:a + c]
                if gate is None:
                    last = dve.tensor_tensor(x, banks[u * n + s][:, 0:c], x, ALU.add)
                else:
                    last = dve.scalar_tensor_tensor(out=x, in0=banks[u * n + s][:, 0:c], scalar=gate(m * per + u, s),
                                                    in1=x, op0=ALU.mult, op1=ALU.add)
        return last
    linear(K, name, w, panels, per * n, features_out(acts, kc, width, spans), kc * width, on_dve=take, first=first)


def route(K, h):
    nc, d = K.nc, K.dram
    with ExitStack() as own:
        def sb(name, *shape):
            return own.enter_context(nc.sbuf_tensor(f"route_{name}", list(shape), F32))
        w, b, logits = sb("w", P, KD, 36), sb("b", 1, 36), sb("logits", P, QT, 36)
        eq, seen, sel, top = sb("eq", P, 8), sb("seen", P, 8), sb("sel", P, 3, 8), sb("top", P, 8)
        gexp, small, gsel, esel = sb("gexp", P, 4), sb("small", P, 8), sb("gsel", P, 4), sb("esel", P, 8)
        comb, combt = sb("comb", P, QT, 32), sb("combt", 32, T)
        here, logit, ready, chain, shifted, exped = (K.sem(f"route_{n}") for n in (
            "here", "logit", "ready", "chain", "shifted", "exped"))
        combed, turned, out, stored = (K.sem(f"route_{n}") for n in ("combed", "turned", "out", "stored"))
        block = own.enter_context(nc.Block())

        @block.sync
        def _(sp):
            sp.dma_start(w[:, :, :], d["w_route"]).then_inc(here, 16)
            sp.dma_start(b[:, :], d["b_route"]).then_inc(here, 16)
            sp.wait_ge(out, 1)
            sp.dma_start(d["comb"], combt[:, :]).then_inc(stored, 16)
            sp.wait_ge(stored, 16)

        @block.tensor
        def _(pe):
            pe.wait_ge(here, 32)
            for q in range(QT):
                for k in range(KD):
                    pe.matmul(K.ps[:, q, 0:36], h[:, k, q * P:(q + 1) * P], w[:, k, :], start=k == 0, stop=False)
                pe.matmul(K.ps[:, q, 0:36], K.ones[0:1, 0:P], b[:, :], start=False, stop=True).then_inc(logit, 1)
            pe.wait_ge(combed, QT)
            for q in range(QT):
                mm = pe.transpose(K.ps[0:32, 4, q * P:(q + 1) * P], comb[:, q, :], K.ident[:, :])
            mm.then_inc(turned, 1)

        @block.scalar
        def _(act):
            for q in range(QT):
                act.wait_ge(shifted, 2 * q + 1)
                act.activation(gexp[:, :], logits[:, q, 0:4], ACT.Exp, bias=small[:, 0:1],
                               accum_out=small[:, 1:2]).then_inc(exped, 1)
                act.wait_ge(shifted, 2 * q + 2)
                act.activation(small[:, 4:5], small[:, 3:4], ACT.Exp).then_inc(exped, 1)

        @block.vector
        def _(dve):
            steps = [0]

            def link(ins):
                steps[0] += 1
                ins.then_inc(chain, 1)
                dve.wait_ge(chain, steps[0])

            def first_of(dst, n):
                link(dve.tensor_tensor_scan(seen[:, 0:n], K.ones[:, 0:n], eq[:, 0:n], 0.0, ALU.mult, ALU.add))
                link(dve.scalar_tensor_tensor(out=dst, in0=seen[:, 0:n], scalar=1.0, in1=eq[:, 0:n],
                                              op0=ALU.is_equal, op1=ALU.mult))

            for q in range(QT):
                dve.wait_ge(logit, q + 1)
                link(dve.tensor_copy(logits[:, q, :], K.ps[:, q, 0:36]))
                g, e = logits[:, q, 0:4], logits[:, q, 4:36]
                link(dve.reduce_max(small[:, 2:3], g, AX))
                dve.tensor_scalar(small[:, 0:1], small[:, 2:3], -1.0, None, ALU.mult).then_inc(shifted, 1)
                link(dve.tensor_scalar(eq[:, 0:4], g, small[:, 2:3], None, ALU.is_equal))
                first_of(gsel[:, :], 4)
                link(dve.tensor_scalar(esel[:, :], e[:, 0:8], gsel[:, 0:1], None, ALU.mult))
                for n in range(1, 4):
                    link(dve.scalar_tensor_tensor(out=esel[:, :], in0=e[:, 8 * n:8 * n + 8], scalar=gsel[:, n:n + 1],
                                                  in1=esel[:, :], op0=ALU.mult, op1=ALU.add))
                link(dve.max(top[:, :], esel[:, :]))
                dve.tensor_tensor(small[:, 3:4], top[:, 1:2], top[:, 0:1], ALU.subtract).then_inc(shifted, 1)
                link(dve.tensor_scalar(eq[:, :], esel[:, :], top[:, 0:1], None, ALU.is_equal))
                first_of(sel[:, 0, :], 8)
                link(dve.scalar_tensor_tensor(out=eq[:, :], in0=esel[:, :], scalar=top[:, 1:2], in1=sel[:, 0, :],
                                              op0=ALU.is_equal, op1=ALU.is_gt))
                first_of(sel[:, 1, :], 8)
                dve.wait_ge(exped, 2 * q + 2)
                link(dve.tensor_scalar(small[:, 5:6], small[:, 4:5], 1.0, small[:, 1:2], ALU.add, ALU.mult))
                link(dve.reciprocal(small[:, 6:7], small[:, 5:6]))
                link(dve.tensor_scalar(sel[:, 2, :], sel[:, 1, :], small[:, 4:5], None, ALU.mult))
                link(dve.tensor_tensor(sel[:, 2, :], sel[:, 2, :], sel[:, 0, :], ALU.add))
                link(dve.tensor_scalar(sel[:, 2, :], sel[:, 2, :], small[:, 6:7], None, ALU.mult))
                for n in range(4):
                    ins = dve.tensor_scalar(comb[:, q, 8 * n:8 * n + 8], sel[:, 2, :], gsel[:, n:n + 1], None, ALU.mult)
                ins.then_inc(combed, 1)
            dve.wait_ge(turned, 1)
            dve.tensor_copy(combt[:, :], K.ps[0:32, 4, :]).then_inc(out, 1)
    K.end()


def experts(K, h):
    nc, d = K.nc, K.dram
    with ExitStack() as own:
        weights = own.enter_context(nc.sbuf_tensor("expert_weights", [P, 2, 3, KD * 256], F32))
        share = own.enter_context(nc.sbuf_tensor("expert_share", [P, 2, T], F32))
        silu = own.enter_context(nc.sbuf_tensor("expert_silu", [P, 2, T], F32))
        hid = own.enter_context(nc.sbuf_tensor("expert_hidden", [P, 2, 2, T], F32))
        up_here = [K.sem(f"moe_up_here{u}") for u in range(2)]
        down_here = [K.sem(f"moe_down_here{u}") for u in range(2)]
        upped = [K.sem(f"moe_upped{u}") for u in range(2)]
        downed = [K.sem(f"moe_downed{u}") for u in range(2)]
        silued, rose, mixed = K.sem("moe_silued"), K.sem("moe_rose"), [K.sem(f"moe_mixed{u}") for u in range(2)]
        added = [K.sem(f"moe_added{u}") for u in range(2)]
        block = own.enter_context(nc.Block())

        @block.sync
        def _(sp):
            with sp.Fori(0, N_EXP // 2) as i:
                for u in range(2):
                    e = i * 2 + u
                    sp.wait_ge(upped[u], i * 2 + 1)
                    for n, name in enumerate(("w_gate", "w_up")):
                        sp.dma_start(weights[:, u, n, :], d[name][e]).then_inc(up_here[u], 16)
                    sp.wait_ge(downed[u], i * 8 + 1)
                    sp.dma_start(weights[:, u, 2, :], d["w_down"][e]).then_inc(down_here[u], 16)
                    sp.wait_ge(mixed[u], i * 2 + 1)
                    sp.dma_start(share[:, u, :], d["comb"][ds(e, 1), :].to_broadcast([P, T])).then_inc(down_here[u], 16)

        @block.tensor
        def _(pe):
            def up(i, u, waits):
                pe.wait_ge(up_here[u], (i + 1) * 32)
                for f in range(2):
                    if waits is not None:
                        pe.wait_ge(mixed[1 - u], waits(f) + 1)
                    for n in range(2):
                        for k in range(KD):
                            mm = pe.matmul(K.ps[:, 2 * n + f, :], weights[:, u, n, k * 256 + f * P:k * 256 + (f + 1) * P],
                                           h[:, k, :], start=k == 0, stop=k == KD - 1)
                    mm.then_inc(upped[u], 1)

            def down(i, u, before):
                pe.wait_ge(down_here[u], (i + 1) * 32)
                pe.wait_ge(mixed[u], (i + 1) * 2 + 1)
                for m in range(KD):
                    if m >= 4:
                        pe.wait_ge(added[u], i * 8 + m - 3)
                    elif before is not None:
                        pe.wait_ge(added[1 - u], before + m)
                    for f in range(2):
                        mm = pe.matmul(K.ps[:, 4 + m % 4, :], weights[:, u, 2, f * D + m * P:f * D + (m + 1) * P],
                                       hid[:, u, f, :], start=f == 0, stop=f == 1)
                    mm.then_inc(downed[u], 1)

            for u in range(2):
                pe.sem_inc(upped[u], 1)
                pe.sem_inc(downed[u], 1)
            up(0, 0, None)
            up(0, 1, lambda f: f + 1)
            down(0, 0, None)
            with pe.Fori(1, N_EXP // 2) as i:
                up(i, 0, lambda f: i * 2 + f - 1)
                down(i - 1, 1, (i - 1) * 8 + 5)
                up(i, 1, lambda f: i * 2 + f + 1)
                down(i, 0, (i - 1) * 8 + 5)
            down(N_EXP // 2 - 1, 1, (N_EXP // 2 - 1) * 8 + 5)

        @block.scalar
        def _(act):
            with act.Fori(0, N_EXP // 2) as i:
                for u in range(2):
                    for f in range(2):
                        act.wait_ge(upped[u], i * 2 + f + 1 + 1)
                        if u:
                            act.wait_ge(mixed[0], i * 2 + f + 1 + 1)
                        else:
                            act.wait_ge(mixed[1], i * 2 + 1)
                        act.activation(silu[:, f, :], K.ps[:, f, :], ACT.Silu).then_inc(silued, 1)

        @block.vector
        def _(dve):
            def mix(i, u, first):
                for f in range(2):
                    n = i * 4 + u * 2 + f
                    dve.wait_ge(silued, n + 1)
                    if not first:
                        dve.wait_ge(downed[u], i * 8 + 1)
                    dve.tensor_tensor(hid[:, u, f, :], K.ps[:, 2 + f, :], silu[:, f, :], ALU.mult).then_inc(rose, 1)
                    dve.wait_ge(down_here[u], (i + 1) * 32)
                    dve.wait_ge(rose, n + 1)
                    dve.tensor_tensor(hid[:, u, f, :], hid[:, u, f, :], share[:, u, :], ALU.mult).then_inc(mixed[u], 1)

            def add(i, u):
                for m in range(KD):
                    dve.wait_ge(downed[u], i * 8 + m + 1 + 1)
                    dve.tensor_tensor(K.x[:, m, 0:T], K.ps[:, 4 + m % 4, :], K.x[:, m, 0:T],
                                      ALU.add).then_inc(added[u], 1)

            for u in range(2):
                dve.sem_inc(mixed[u], 1)
            mix(0, 0, True)
            mix(0, 1, True)
            add(0, 0)
            with dve.Fori(1, N_EXP // 2) as i:
                mix(i, 0, False)
                add(i - 1, 1)
                mix(i, 1, False)
                add(i, 0)
            add(N_EXP // 2 - 1, 1)
    K.end()


def embed_gate(K, h):
    nc, d = K.nc, K.dram
    with ExitStack() as own:
        p = own.enter_context(nc.sbuf_tensor("ple", [P, 2, T], F32))
        parts = K.two(own, "ple_parts", [2, T])
        gate = own.enter_context(nc.sbuf_tensor("ple_gate", [P, PAIR, T], F32))
        gated = own.enter_context(nc.sbuf_tensor("ple_gated", [P, PAIR, T], F32))
        load(K, "load_p", [(p[:, :, :], d["p"])])
        split(K, "split_p", [(p[:, k, :], parts[:, k, :]) for k in range(2)])
        own_product = K.sem("ple_product")

        def groups(slot):
            return [(0, 0, T, P, [(slot[:, k * P:(k + 1) * P], h[:, k, :]) for k in range(KD)]),
                    (1, 0, T, P, [(slot[:, (KD + k) * P:(KD + k + 1) * P], parts[:, k, :]) for k in range(2)])]

        def sigmoid(act, m, banks, j):
            return act.activation(gate[:, j, :], banks[0], ACT.Sigmoid)

        def take(dve, m, banks, j):
            dve.tensor_tensor(gated[:, j, :], gate[:, j, :], banks[1], ALU.mult).then_inc(own_product, 1)
            dve.wait_ge(own_product, m + 1)
            return dve.tensor_tensor(K.x[:, m, 0:T], K.x[:, m, 0:T], gated[:, j, :], ALU.add)
        linear(K, "ple", d["w_ple"], KD, 2, groups, 10 * P, on_act=sigmoid, on_dve=take)


def first_block(K):
    nc, d = K.nc, K.dram
    with ExitStack() as own:
        gates = own.enter_context(nc.sbuf_tensor("gates", [P, 2 * KD, T], F32))
        heads_out = own.enter_context(nc.sbuf_tensor("heads_out", [P, KD, T], F32))
        with ExitStack() as here:
            proj = here.enter_context(nc.sbuf_tensor("projected", [P, 18, T], F32))
            vb = here.enter_context(nc.sbuf_tensor("v_b", [P, QT, 512], F32))
            widx = here.enter_context(nc.sbuf_tensor("w_idx", [P, QT * 8], F32))
            with ExitStack() as norm:
                h = norm_model(K, norm, "attn_norm", LAT, lambda i, k: K.v("attn_norm", k))
                project_in(K, h, proj, gates, vb, widx)
            masks = here.enter_context(nc.sbuf_tensor("masks", [P, 4, P], F32))
            load(K, "load_masks", [(masks[:, :, :], d["masks"])])
            K.scratch(here, "attention_scratch", 20 * T)
            K.bias = K.flat[:, 12 * T:20 * T].rearrange("p (h n) -> p h n", h=HEADS)
            sparse_attention(K, proj, widx, masks[:, 0, :], heads_out)
            stick_breaking(K, proj, vb, masks[:, 1, :], masks[:, 2, :], masks[:, 3, :], heads_out)
        merge(K, heads_out, gates)
    with ExitStack() as own:
        h = own.enter_context(nc.sbuf_tensor("ffn_normed", [P, KD, T], F32))
        rms(K, "ffn_norm", [([K.x[:, k, 0:T] for k in range(KD)], [h[:, k, :] for k in range(KD)], T)], D,
            lambda i, k: K.v("ffn_norm", k))
        route(K, h)
        experts(K, h)
    with ExitStack() as own:
        h = norm_model(K, own, "ple_norm", LAT, lambda i, k: K.v("ple_norm", k))
        embed_gate(K, h)
    rms(K, "final_norm", [([K.x[:, k, 0:T] for k in range(KD)], [K.x[:, k, 0:T] for k in range(KD)], T)], D,
        lambda i, k: K.v("final_norm", k))



SHIFT1, SCALE1, GATE1, SHIFT2, SCALE2, GATE2 = (KD * n for n in range(6))


def modulations(K):
    nc, d = K.nc, K.dram
    with ExitStack() as own:
        cs = own.enter_context(nc.sbuf_tensor("silu_c", [P, KD, 2], F32))
        with nc.Block() as block:
            @block.scalar
            def _(act):
                for s, name in enumerate(("c_lat", "c_ctx")):
                    at = VEC_AT[name][0]
                    act.activation(cs[:, :, s], K.vec[:, at:at + KD], ACT.Silu)

        def groups(slot):
            return [(0, w * 2, 2, P, [(slot[:, k * 256 + w * P:k * 256 + (w + 1) * P], cs[:, k, :])
                                      for k in range(KD)]) for w in range(2)]
        for layer in range(2):
            def take(dve, m, banks, j, layer=layer):
                for w in range(2):
                    at = VEC_AT[f"b_ada_{layer}"][0]
                    last = dve.tensor_scalar(K.mod[:, layer, m * 2 + w, :], banks[0][:, w * 2:w * 2 + 2],
                                             K.vec[:, ds(m * 2 + (at + w), 1)], None, ALU.add)
                return last
            linear(K, f"ada{layer}", d[f"ada_{layer}"], 24, 2, groups, 2048, on_dve=take,
                   split=False)
    with nc.Block() as block:
        @block.vector
        def _(dve):
            for layer in range(2):
                for n, scale in enumerate((SCALE1, SCALE2)):
                    at = VEC_AT[f"norm{n + 1}_{layer}"][0]
                    dve.scalar_tensor_tensor(out=K.gain[:, layer, n, :, :], in0=K.mod[:, layer, scale:scale + KD, :],
                                             scalar=1.0, op0=ALU.add, op1=ALU.mult,
                                             in1=K.vec[:, at:at + KD].unsqueeze(2).to_broadcast([P, KD, 2]))


def norm_modulated(K, own, layer, n, spans, room=None):
    shift = (SHIFT1, SHIFT2)[n]
    return norm_model(K, own, f"norm{n}_{layer}", spans, lambda i, k: K.gain[:, layer, n, k, i:i + 1],
                      lambda i, k: K.mod[:, layer, shift + k, i:i + 1], room)


HALF = KF // 2


def feed_forward(K, layer, spans):
    n = len(spans)
    with ExitStack() as own:
        h = norm_modulated(K, own, layer, 1, spans)
        hid = K.two(own, f"ff_hidden{layer}", [HALF, N])
        silu = own.enter_context(K.nc.sbuf_tensor(f"ff_silu{layer}", [P, PAIR, N], F32))
        rose = own.enter_context(K.nc.sbuf_tensor(f"ff_rose{layer}", [P, PAIR, N], F32))
        for part in range(2):
            timed, high = K.sem("ff_timed"), K.sem("ff_high")

            def gate(act, m, banks, j):
                for s, (a, c) in enumerate(spans):
                    last = act.activation(silu[:, j, a:a + c], banks[s][:, 0:c], ACT.Silu)
                return last

            def take(dve, m, banks, j):
                for s, (a, c) in enumerate(spans):
                    ins = dve.tensor_tensor(rose[:, j, a:a + c], banks[n + s][:, 0:c], silu[:, j, a:a + c], ALU.mult)
                ins.then_inc(timed, 1)
                dve.wait_ge(timed, m + 1)
                w = spans[-1][0] + spans[-1][1]
                dve.tensor_copy(hid.high[:, m, 0:w], rose[:, j, 0:w]).then_inc(high, 1)
                dve.wait_ge(high, m + 1)
                return dve.tensor_tensor(hid.low[:, m, 0:w], rose[:, j, 0:w], hid.high[:, m, 0:w].bitcast(F32),
                                         ALU.subtract)
            linear(K, f"ff_up{layer}{part}", K.dram[f"w13_{layer}"], HALF, 2 * n, features_out(h, KD, 256, spans), 2048,
                   on_act=gate, on_dve=take, first=part * HALF)
            residual(K, f"ff_down{layer}{part}", K.dram[f"w2_{layer}"], KD, hid, HALF, P, spans,
                     lambda k, s: K.mod[:, layer, k + GATE2, s:s + 1], first=part * KD)


def rotate(K, pairs, cos, sin, rot):
    nc = K.nc
    made, spun, sined, cosed = (K.sem(f"rope_{n}") for n in ("made", "spun", "sined", "cosed"))
    with ExitStack() as own:
        tmp = own.enter_context(nc.sbuf_tensor("rope_tmp", [64, 2, T], F32))
        block = own.enter_context(nc.Block())

        @block.tensor
        def _(pe):
            for n, t in enumerate(pairs):
                if n >= 4:
                    pe.wait_ge(sined, n - 3)
                pe.matmul(K.ps[0:64, n % 4, :], rot, t, start=True, stop=True).then_inc(made, 1)

        @block.vector
        def _(dve):
            for n, t in enumerate(pairs):
                dve.wait_ge(made, n + 1)
                dve.tensor_tensor(tmp[:, n % 2, :], K.ps[0:64, n % 4, :], sin, ALU.mult).then_inc(sined, 1)
                dve.tensor_tensor(t, t, cos, ALU.mult).then_inc(cosed, 1)
                dve.wait_ge(sined, n + 1)
                dve.wait_ge(cosed, n + 1)
                dve.tensor_tensor(t, t, tmp[:, n % 2, :], ALU.add)
    K.end()


def latent_attention(K):
    nc, d = K.nc, K.dram
    with ExitStack() as outer:
        qn = outer.enter_context(nc.sbuf_tensor("q_nope", [P, HEADS, N], F32))
        with ExitStack() as own:
            latent_heads(K, own, qn)
        residual_of(K, "mla_out", d["mla_out"], 4, qn, KD, 256, BOTH, lambda k, s: K.mod[:, 0, k + GATE1, s:s + 1])


def latent_heads(K, own, qn):
    nc, d = K.nc, K.dram
    low = own.enter_context(nc.sbuf_tensor("low_rank", [P, 6, N], F32))
    kr = low[0:64, 5, :]
    with ExitStack() as norm:
        h = norm_modulated(K, norm, 0, 0, BOTH, qn)

        def take(dve, m, banks, j):
            for s, (a, c) in enumerate(BOTH):
                last = dve.tensor_copy(low[:, m, a:a + c], banks[s][:, 0:c])
            return last
        linear(K, "mla_in", d["mla_in"], 6, 2, features_out(h, KD, P, BOTH), KD * P, on_dve=take)

    kn = own.enter_context(nc.sbuf_tensor("k_nope", [P, HEADS, N], F32))
    qr = own.enter_context(nc.sbuf_tensor("q_rope", [64, HEADS, N], F32))
    v = own.enter_context(nc.sbuf_tensor("values", [P, N // P, HEADS * P], F32))

    def chunks(ap, which, rows=P):
        return [([ap[0:rows, k, a:a + c] for k in which], [ap[0:rows, k, a:a + c] for k in which], c)
                for a, c in BOTH]
    rms(K, "mla_q_norm", chunks(low, range(3)), 384, lambda i, k: K.v("q_norm", k))
    rms(K, "mla_kv_norm", chunks(low, (3, 4)), 256, lambda i, k: K.v("mkv_norm", k))
    rms(K, "mla_kr_norm", chunks(low, (5,), 64), 64, lambda i, k: K.v("kr", 0, 64), rows=64)
    with ExitStack() as here:
        lows = K.two(here, "low_rank_parts", [5, N])
        split(K, "split_low", [(low[:, k, :], lows[:, k, :]) for k in range(5)])

        def q_out(slot):
            return [(2 * w + s, 0, c, P, [(slot[:, k * 256 + w * P:k * 256 + (w + 1) * P], lows[:, k, a:a + c])
                                          for k in range(3)]) for w in range(2) for s, (a, c) in enumerate(BOTH)]

        def take_qr(act, m, banks, j):
            for s, (a, c) in enumerate(BOTH):
                last = act.activation(qr[:, m, a:a + c], banks[2 + s][0:64, 0:c], ACT.Copy)
            return last

        def take_qn(dve, m, banks, j):
            for s, (a, c) in enumerate(BOTH):
                last = dve.tensor_copy(qn[:, m, a:a + c], banks[s][:, 0:c])
            return last
        linear(K, "mla_q", d["mla_uq"], HEADS, 4, q_out, 768, on_act=take_qr, on_dve=take_qn)

        def kv_out(slot):
            out = [(s, 0, c, P, [(slot[:, k * 256:k * 256 + P], lows[:, 3 + k, a:a + c]) for k in range(2)])
                   for s, (a, c) in enumerate(BOTH)]
            return out + [(2 + t // 4, (t % 4) * P, P, P,
                           [(lows[:, 3 + k, t * P:(t + 1) * P], slot[:, k * 256 + P:(k + 1) * 256])
                            for k in range(2)]) for t in range(N // P)]

        def take_v(act, m, banks, j):
            for b, t, n in ((2, 0, 4), (3, 4, 2)):
                last = act.activation(v[:, t:t + n, ds(m * P, P)],
                                      banks[b][:, 0:n * P].rearrange("p (t e) -> p t e", t=n), ACT.Copy)
            return last

        def take_kn(dve, m, banks, j):
            for s, (a, c) in enumerate(BOTH):
                last = dve.tensor_copy(kn[:, m, a:a + c], banks[s][:, 0:c])
            return last
        linear(K, "mla_kv", d["mla_ukv"], HEADS, 4, kv_out, 512, on_act=take_v, on_dve=take_kn)

    rope = own.enter_context(nc.sbuf_tensor("rope", [64, 2, T], F32))
    rot = own.enter_context(nc.sbuf_tensor("rot", [64, 64], F32))
    load(K, "load_rope", [(rope[:, :, :], d["rope"]), (rot[:, :], d["rot"])])

    def heads(ap, rows=P):
        return [([ap[0:rows, h, a:a + c]], [ap[0:rows, h, a:a + c]], c) for h in range(HEADS) for a, c in BOTH]
    rms(K, "mla_qn", heads(qn), P, lambda i, k: K.v("qn"))
    rms(K, "mla_kn", heads(kn), P, lambda i, k: K.v("kn"))
    rms(K, "mla_qr", heads(qr, 64), 64, lambda i, k: K.v("qr", 0, 64), rows=64)
    rotate(K, [qr[:, h, 0:T] for h in range(HEADS)] + [kr[:, 0:T]], rope[:, 0, :], rope[:, 1, :], rot[:, :])

    tasks = []
    for h in range(HEADS):
        for i in range(N // P):
            k0 = 0 if i < QT else QT
            q = slice(i * P, (i + 1) * P)
            tasks.append((h, N - k0 * P, [(qn[:, h, q], kn[:, h, k0 * P:N]), (qr[:, h, q], kr[:, k0 * P:N])],
                          k0, i * P, None, None))

    def values(h, turn):
        vh = [v[:, t, h * P:(h + 1) * P] for t in range(N // P)]
        return [(6, 0, T, [(vh[t], turn[:, t, 0:T], 0) for t in range(N // P)]),
                (7, 0, C, [(vh[t], turn[:, t, T:N], 0) for t in range(QT, N // P)])]
    K.scratch(own, "mla_scratch", 2 * (N // P) * N + 2 * N)
    attend(K, "mla", tasks, (N // P, N, N), HEADS, 192 ** -0.5, values,
           lambda h: [(qn[:, h, 0:T], 6, T), (qn[:, h, T:N], 7, C)])


LEVELS = 7
CH = N // P
ORDER = ([4, 5, 0, 1, 2, 3], [5, 4, 3, 2, 1, 0])
LAST = (P - 1, 0)


HG_WORDS = 2 * (3 * N + 2 * T + 9 * P) + 2 * N + LEVELS * T


def recurrence(K, sig, q, inp, lb, masks):
    nc = K.nc
    f = K.flat
    at = [0]

    def part(n):
        at[0] += n
        return f[:, at[0] - n:at[0]]
    kp = [part(N) for _ in range(2)]
    dec = [part(N) for _ in range(2)]
    key = [part(N) for _ in range(2)]
    qd = [part(T) for _ in range(2)]
    att = [part(T).rearrange("p (c t) -> p c t", c=QT) for _ in range(2)]
    state = [part(4 * P).rearrange("p (c t) -> p c t", c=4) for _ in range(2)]
    knat = [part(5 * P).rearrange("p (c t) -> p c t", c=5) for _ in range(2)]
    vh = part(N).rearrange("p (c t) -> p c t", c=CH)
    vt = part(N)
    lev = part(LEVELS * T).rearrange("p (l n) -> p l n", l=LEVELS)
    names = ("f", "ln", "scan", "key", "lastdiff", "lastexp", "qexp", "kprime", "qdec", "turned", "knat", "diffed",
             "exped", "grown", "product", "picked", "stated", "spread", "valued", "outed", "vstaged", "vturned", "vcopied", "zeroed", "clear")
    S = {n: K.sem(f"hg_{n}") for n in names}
    STEPS, PRODUCTS, STATES = 2 * LEVELS, 2 * (LEVELS + 1), 10

    def halves(ap, l):
        v = ap.rearrange("p (b s n) -> p b s n", s=2, n=P >> (l + 1))
        return v

    def sides(ap, l, r):
        v = halves(ap, l)
        return (v[:, :, 1, :], v[:, :, 0, :]) if r == 0 else (v[:, :, 0, :], v[:, :, 1, :])

    def middle(ap, l, r):
        n = P >> (l + 1)
        v = halves(ap, l)
        m = v[:, :, 0, n - 1:n] if r == 0 else v[:, :, 1, 0:1]
        return m.to_broadcast([P, T >> (LEVELS - l), n])

    with ExitStack() as own:
        elast = own.enter_context(nc.sbuf_tensor("hg_elast", [P, 2, CH], F32))
        block = own.enter_context(nc.Block())

        @block.gpsimd
        def _(pool):
            for n in ("lastdiff", "diffed"):
                pool.sem_inc(S[n], 1)
            with pool.Fori(0, HEADS) as i:
                pool.wait_ge(S["vturned"], i + 1)
                pool.tensor_copy(vt, inp[:, i, :]).then_inc(S["vstaged"], 1)
                for r in range(2):
                    pool.wait_ge(S["scan"], i * 2 + r + 1 + 1)
                    d3 = dec[r].rearrange("p (c t) -> p c t", c=CH)
                    pool.tensor_tensor(kp[r].rearrange("p (c t) -> p c t", c=CH),
                                       d3[:, :, LAST[r]:LAST[r] + 1].to_broadcast([P, CH, P]), d3,
                                       ALU.subtract).then_inc(S["lastdiff"], 1)
                    for l in range(LEVELS):
                        pool.wait_ge(S["product"], i * PRODUCTS + (l + 2 if r else 0) + 1)
                        dq, dk = sides(dec[r][:, 0:T], l, r)
                        eq, ek = sides(lev[:, l, :], l, r)
                        pool.tensor_tensor(eq, dq, middle(dec[r][:, 0:T], l, r), ALU.subtract)
                        pool.tensor_tensor(ek, middle(dec[r][:, 0:T], l, r), dk, ALU.subtract).then_inc(S["diffed"], 1)

        @block.scalar
        def _(act):
            act.preload_act_table_set(LOG_EXP)
            for n in ("ln", "qexp", "lastexp", "exped", "knat", "outed", "vcopied"):
                act.sem_inc(S[n], 1)
            with act.Fori(0, HEADS) as i:
                act.wait_ge(S["valued"], i + 1)
                act.wait_ge(S["vturned"], i + 1 + 1)
                act.activation(vh.rearrange("p c t -> p (c t)"), K.psf[:, 4 * BANK:4 * BANK + N],
                               ACT.Copy).then_inc(S["vcopied"], 1)
                for r in range(2):
                    act.wait_ge(S["f"], i * 2 + r + 1 + 1)
                    act.activation(kp[r], kp[r], ACT.Ln).then_inc(S["ln"], 1)
                for r in range(2):
                    act.wait_ge(S["scan"], i * 2 + r + 1 + 1)
                    act.activation(qd[r], dec[r][:, 0:T], ACT.Exp)
                    act.activation(elast[:, r, :], dec[r].rearrange("p (c t) -> p c t", c=CH)[:, :, LAST[r]],
                                   ACT.Exp).then_inc(S["qexp"], 1)
                    act.wait_ge(S["lastdiff"], i * 2 + r + 1 + 1)
                    act.activation(kp[r], kp[r], ACT.Exp).then_inc(S["lastexp"], 1)
                    for l in range(LEVELS):
                        act.wait_ge(S["diffed"], i * STEPS + r * LEVELS + l + 1 + 1)
                        act.activation(lev[:, l, :], lev[:, l, :], ACT.Exp).then_inc(S["exped"], 1)
                    act.wait_ge(S["turned"], i * 2 + r + 1 + 1)
                    act.activation(knat[r].rearrange("p c t -> p (c t)"), K.psf[:, 4 * BANK:4 * BANK + 5 * P],
                                   ACT.Copy).then_inc(S["knat"], 1)
                act.wait_ge(S["valued"], i + 1 + 1)
                act.activation(q[:, i, :], K.ps[:, 7, :], ACT.Copy).then_inc(S["outed"], 1)

        @block.tensor
        def _(pe):
            def states(i, r):
                pe.wait_ge(S["vcopied"], i + 1 + 1)
                pe.wait_ge(S["knat"], i * 2 + r + 1 + 1)
                pe.wait_ge(S["spread"], i * STATES + r * 5 + 1)
                pe.wait_ge(S["outed"], i + 1)
                for n in range(5):
                    mm = pe.matmul(K.psf[:, 6 * BANK + n * P:6 * BANK + (n + 1) * P], knat[r][:, n, :],
                                   vh[:, ORDER[r][n], :], start=True, stop=True)
                mm.then_inc(S["stated"], 1)

            for n in ("turned", "product", "stated", "valued", "vturned"):
                pe.sem_inc(S[n], 1)
            with pe.Fori(0, HEADS) as i:
                pe.wait_ge(S["knat"], i * 2 + 1)
                pe.wait_ge(S["vstaged"], i + 1)
                for c in range(CH):
                    mm = pe.transpose(K.psf[:, 4 * BANK + c * P:4 * BANK + (c + 1) * P],
                                      vt[:, c * P:(c + 1) * P], K.ident[:, :])
                mm.then_inc(S["vturned"], 1)
                for r in range(2):
                    p0 = r * (LEVELS + 1)
                    pe.wait_ge(S["key"], i * 2 + r + 1 + 1)
                    pe.wait_ge(S["picked"], i * PRODUCTS + max(p0 - 3, 0) + 1)
                    for c in range(QT):
                        mm = pe.matmul(K.ps[:, p0 % 4, c * P:(c + 1) * P], key[r][:, c * P:(c + 1) * P],
                                       q[:, i, c * P:(c + 1) * P], start=True, stop=True)
                    mm.then_inc(S["product"], 1)
                    pe.wait_ge(S["kprime"], i * 2 + r + 1 + 1)
                    if r:
                        pe.wait_ge(S["knat"], i * 2 + r + 1)
                    else:
                        pe.wait_ge(S["vcopied"], i + 1 + 1)
                    for n in range(5):
                        c = ORDER[r][n]
                        mm = pe.transpose(K.psf[:, 4 * BANK + n * P:4 * BANK + (n + 1) * P],
                                          kp[r][:, c * P:(c + 1) * P], K.ident[:, :])
                    mm.then_inc(S["turned"], 1)
                    for l in range(LEVELS):
                        p = p0 + 1 + l
                        pe.wait_ge(S["grown"], i * STEPS + r * LEVELS + l + 1 + 1)
                        pe.wait_ge(S["picked"], i * PRODUCTS + max(p - 3, 0) + 1)
                        for c in range(QT):
                            g = lev[:, l, c * P:(c + 1) * P]
                            mm = pe.matmul(K.ps[:, p % 4, c * P:(c + 1) * P], g, g, start=True, stop=True)
                        mm.then_inc(S["product"], 1)
                    states(i, r)
                pe.wait_ge(S["picked"], (i + 1) * PRODUCTS + 1)
                pe.wait_ge(S["spread"], (i + 1) * STATES + 1)
                pe.wait_ge(S["outed"], i + 1)
                pe.wait_ge(S["qdec"], (i + 1) * 2 + 1)
                for c in range(QT):
                    terms = []
                    for r in range(2):
                        terms.append((vh[:, c, :], att[r][:, c, :]))
                        terms.append((state[r][:, ORDER[r].index(c) - 2, :], qd[r][:, c * P:(c + 1) * P]))
                    for t, (a, b) in enumerate(terms):
                        mm = pe.matmul(K.ps[:, 7, c * P:(c + 1) * P], a, b, start=t == 0, stop=t == 3)
                mm.then_inc(S["valued"], 1)

        @block.vector
        def _(dve):
            for r in range(2):
                dve.memset(att[r].rearrange("p c t -> p (c t)"), 0.0).then_inc(S["zeroed"], 1)
            dve.wait_ge(S["zeroed"], 2)
            for n in ("f", "scan", "key", "kprime", "qdec", "grown", "picked", "spread"):
                dve.sem_inc(S[n], 1)
            with dve.Fori(0, HEADS) as i:
                for r in range(2):
                    dve.wait_ge(S["turned"], i * 2 + 1)
                    dve.tensor_scalar(kp[r], sig[:, r * HEADS + i, :], lb[:, 1, ds(i + r * HEADS, 1)],
                                      lb[:, 0, ds(i + r * HEADS, 1)], ALU.mult, ALU.add).then_inc(S["f"], 1)
                for r in range(2):
                    dve.wait_ge(S["ln"], i * 2 + r + 1 + 1)
                    dve.wait_ge(S["diffed"], i * STEPS + 1)
                    dve.wait_ge(S["qexp"], i * 2 + 1)
                    for c in range(CH):
                        step = slice(c * P, (c + 1) * P)
                        d, lf = dec[r][:, step], kp[r][:, step]
                        if r:
                            d, lf = d[:, ::-1], lf[:, ::-1]
                        ins = dve.tensor_tensor_scan(d, K.ones[:, :], lf, 0.0, ALU.mult, ALU.add)
                    ins.then_inc(S["scan"], 1)
                    dve.wait_ge(S["product"], i * PRODUCTS + 1)
                    dve.tensor_scalar(key[r], sig[:, r * HEADS + i, :], lb[:, 2, ds(i + r * HEADS, 1)],
                                      lb[:, 1, ds(i + r * HEADS, 1)], ALU.mult, ALU.add).then_inc(S["key"], 1)
                for r in range(2):
                    dve.wait_ge(S["lastexp"], i * 2 + r + 1 + 1)
                    dve.wait_ge(S["key"], i * 2 + r + 1 + 1)
                    dve.tensor_tensor(kp[r], kp[r], key[r], ALU.mult).then_inc(S["kprime"], 1)
                    dve.tensor_tensor(qd[r], qd[r], q[:, i, :], ALU.mult).then_inc(S["qdec"], 1)

                    def grow(l):
                        dve.wait_ge(S["exped"], i * STEPS + r * LEVELS + l + 1 + 1)
                        eq, ek = sides(lev[:, l, :], l, r)
                        qq, _ = sides(q[:, i, :], l, r)
                        _, kk = sides(key[r][:, 0:T], l, r)
                        dve.tensor_tensor(eq, eq, qq, ALU.mult)
                        dve.tensor_tensor(ek, ek, kk, ALU.mult).then_inc(S["grown"], 1)

                    def pick(p):
                        dve.wait_ge(S["product"], i * PRODUCTS + r * (LEVELS + 1) + p + 1 + 1)
                        dve.wait_ge(S["picked"], i * PRODUCTS + r * (LEVELS + 1) + p + 1)
                        dve.sem_inc(S["clear"], 1)
                        mask = masks[:, r, p, :].unsqueeze(1).to_broadcast([P, QT, P])
                        dve.copy_predicated(att[r], mask, K.ps[:, (r * (LEVELS + 1) + p) % 4, :].rearrange(
                            "p (c t) -> p c t", c=QT)).then_inc(S["picked"], 1)

                    dve.wait_ge(S["valued"], i + 1)
                    grow(0)
                    pick(0)
                    for l in range(LEVELS):
                        if l + 1 < LEVELS:
                            grow(l + 1)
                        pick(l + 1)
                    for n in range(5):
                        c = ORDER[r][n]
                        m = max(n - 1, 0)
                        product = K.psf[:, 6 * BANK + n * P:6 * BANK + (n + 1) * P]
                        dve.wait_ge(S["stated"], i * 2 + r + 1 + 1)
                        if n:
                            dve.wait_ge(S["spread"], i * STATES + r * 5 + n + 1)
                            src = state[r][:, max(n - 2, 0), :]
                            dve.scalar_tensor_tensor(out=state[r][:, m, :], in0=src, scalar=elast[:, r, c:c + 1],
                                                     in1=product, op0=ALU.mult, op1=ALU.add).then_inc(S["spread"], 1)
                        else:
                            dve.tensor_copy(state[r][:, 0, :], product).then_inc(S["spread"], 1)
    K.end()


def gated_recurrence(K):
    nc, d = K.nc, K.dram
    with ExitStack() as outer:
        q = outer.enter_context(nc.sbuf_tensor("hg_q", [P, HEADS, T], F32))
        with ExitStack() as own:
            recurrent_heads(K, own, q)
        residual_of(K, "hg_out", d["hg_out"], 4, q, KD, 256, LAT, lambda k, s: K.mod[:, 1, k + GATE1, s:s + 1])


def recurrent_heads(K, own, q):
    nc, d = K.nc, K.dram
    sig = own.enter_context(nc.sbuf_tensor("hg_sigmoid", [P, 2 * HEADS, N], F32))
    g = own.enter_context(nc.sbuf_tensor("hg_gate", [P, HEADS, T], F32))
    inp = own.enter_context(nc.sbuf_tensor("hg_input", [P, HEADS, N], F32))
    with ExitStack() as norm:
        h = norm_modulated(K, norm, 1, 0, BOTH, sig)

        def sigmoids(act, m, banks, j):
            for s, (a, c) in enumerate(BOTH):
                last = act.activation(sig[:, m, a:a + c], banks[s][:, 0:c], ACT.Sigmoid)
            return last
        linear(K, "hg_z", d["hg_in"], 16, 2, features_out(h, KD, P, BOTH), 1024, on_act=sigmoids)
        lat = features_out(h, KD, P, LAT)
        linear(K, "hg_q", d["hg_in"], 8, 1, lat, 1024, first=16,
               on_dve=lambda dve, m, banks, j: dve.tensor_copy(q[:, m, :], banks[0]))
        linear(K, "hg_g", d["hg_in"], 8, 1, lat, 1024, first=24,
               on_act=lambda act, m, banks, j: act.activation(g[:, m, :], banks[0], ACT.Silu))

        def take_i(dve, m, banks, j):
            for s, (a, c) in enumerate(BOTH):
                last = dve.tensor_copy(inp[:, m, a:a + c], banks[s][:, 0:c])
            return last
        linear(K, "hg_i", d["hg_in"], 8, 2, features_out(h, KD, P, BOTH), 1024, on_dve=take_i, first=32)
    lb = own.enter_context(nc.sbuf_tensor("hg_lb", [P, 3, 2 * HEADS], F32))
    masks = own.enter_context(nc.sbuf_tensor("hg_masks", [P, 2, LEVELS + 1, P], U32))
    load(K, "load_levels", [(masks[:, :, :, :], d["levels"])])
    a0, a1 = VEC_AT["lb0_f"][0], VEC_AT["lb1_f"][0]
    subbed = K.sem("lb_sub")
    sided = K.sem("lb_side")
    with nc.Block() as block:
        @block.vector
        def _(dve):
            dve.tensor_tensor(lb[:, 2, :], K.vec[:, a1:a1 + 2 * HEADS], K.vec[:, a0:a0 + 2 * HEADS],
                              ALU.subtract).then_inc(subbed, 1)
            dve.wait_ge(sided, 2)
            dve.tensor_scalar(lb[:, 2, :], lb[:, 1, :], -1.0, None, ALU.mult)

        @block.scalar
        def _(act):
            act.wait_ge(subbed, 1)
            act.activation(lb[:, 0, :], lb[:, 2, :], ACT.Sigmoid).then_inc(sided, 1)
            act.activation(lb[:, 1, :], lb[:, 2, :], ACT.Sigmoid, scale=-1.0).then_inc(sided, 1)
    K.end()
    with ExitStack() as here:
        K.scratch(here, "hg_scratch", HG_WORDS)
        recurrence(K, sig, q, inp, lb, masks)
    heads = [[q[:, h, :]] for h in range(HEADS)]
    rms(K, "hg_norm", [(x, x, T) for x in heads], P, lambda i, k: K.v("o_norm"))
    with nc.Block() as block:
        @block.vector
        def _(dve):
            for h in range(HEADS):
                dve.tensor_tensor(q[:, h, :], q[:, h, :], g[:, h, :], ALU.mult)


def second_block(K):
    modulations(K)
    latent_attention(K)
    feed_forward(K, 0, BOTH)
    gated_recurrence(K)
    feed_forward(K, 1, LAT)


def start(K):
    d = K.dram
    with K.nc.Block() as block:
        here = K.sem("start_here")

        @block.sync
        def _(sp):
            for dst, src in ((K.x[:, :, 0:T], d["x"]), (K.x[:, :, T:N], d["ctx"]), (K.vec[:, :], d["vec"]),
                             (K.ident[:, :], d["ident"])):
                sp.dma_start(dst, src).then_inc(here, 16)
            sp.wait_ge(here, 64)

        @block.vector
        def _(dve):
            dve.memset(K.ones[:, :], 1.0)
            dve.memset(K.eps[:, :], EPS)
    K.end()


def program(nc, dram, out, upto=99, dump=None):
    with ExitStack() as ctx:
        K = Chip(nc, ctx, dram)
        start(K)
        if upto != 2:
            first_block(K)
        if upto != 1:
            second_block(K)
        stored = nc.alloc_semaphore("out_stored")
        with nc.Block() as block:
            @block.sync
            def _(sp):
                sp.dma_start(out, K.x[:, :, 0:T]).then_inc(stored, 16)
                sp.wait_ge(stored, 16)


def panels(w, width):
    kin, kout = w.shape
    return np.ascontiguousarray(
        w.reshape(kin // P, P, kout // width, width).transpose(2, 1, 0, 3).reshape(kout // width, P, -1))


def tokens_last(x):
    t, f = x.shape
    return np.ascontiguousarray(x.T.reshape(f // P, P, t).transpose(1, 0, 2))


def buckets():
    dist = np.maximum(T - 1 - np.arange(SKEW), 0)
    large = 16 + (np.log(np.maximum(dist, 1).astype(np.float32) / 16) / np.float32(np.log(8.0)) * 16).astype(np.int32)
    bucket = np.where(dist < 16, dist, np.minimum(large, 31))
    return (bucket[None, :] == np.arange(32)[:, None]).astype(np.float32)


def rope_tables():
    pos = np.arange(T)
    inv = (10000.0 ** (-np.arange(0, 32, 2, dtype=np.float32) / 32)).astype(np.float32)
    row = (pos // 64).astype(np.float32)[:, None] * inv
    col = (pos % 64).astype(np.float32)[:, None] * inv
    ang = np.concatenate([row, row, col, col], -1)
    rot = np.zeros((64, 64), np.float32)
    for j in range(16):
        rot[16 + j, j], rot[j, 16 + j] = -1, 1
        rot[48 + j, 32 + j], rot[32 + j, 48 + j] = -1, 1
    return np.ascontiguousarray(np.stack([np.cos(ang).T, np.sin(ang).T], 1)).astype(np.float32), rot


def level_masks():
    s, t = np.arange(P)[:, None], np.arange(P)[None, :]
    out = np.zeros((P, 2, LEVELS + 1, P), np.uint32)
    for r in range(2):
        out[:, r, 0] = s == t
        for l in range(LEVELS):
            n = P >> (l + 1)
            parted = (s // (2 * n) == t // (2 * n)) & (s // n != t // n)
            out[:, r, 1 + l] = parted & ((s < t) if r == 0 else (s > t))
    return out


def arrange(a):
    a = {k: np.asarray(v) for k, v in a.items()}
    w_in = a["w_in"][0]
    col = dict(q_a=(0, 512), c_kv=(512, 640), q_idx=(640, 1152), k_idx=(1152, 1216), w_idx=(1216, 1224),
               q_b=(1224, 1736), k_b=(1736, 2248), v_b=(2248, 2760), gate_a=(2760, 3784), gate_b=(3784, 4808))
    part = {k: w_in[:, x:y] for k, (x, y) in col.items()}
    o = {}
    o["x"] = tokens_last(a["x"][0])
    o["ctx"] = tokens_last(a["ctx_2"][0])
    o["p"] = tokens_last(a["p"][0, 0])
    o["w_main"] = panels(np.concatenate([part[k] for k in (
        "q_a", "c_kv", "k_idx", "k_idx", "q_idx", "q_b", "k_b", "gate_a", "gate_b")], 1), 256)
    o["w_vb"] = panels(part["v_b"], 256)
    o["w_idx"] = panels(part["w_idx"], 8)
    o["w_uk"] = np.ascontiguousarray(a["w_uk"][0].transpose(0, 2, 1).reshape(4, 2, HD, P).transpose(1, 2, 0, 3).reshape(P, 4, P))
    o["w_uv"] = np.ascontiguousarray(a["w_uv"][0].transpose(1, 0, 2))
    o["rel_bias"] = a["rel_bias"]
    o["buckets"] = buckets()
    ab = np.stack([a["w_branch_a"][0], a["w_branch_b"][0]]).reshape(2, 4, P, KD, P)
    o["w_branches"] = np.ascontiguousarray(ab.transpose(3, 2, 0, 1, 4).reshape(KD, P, -1))
    o["w_out"] = panels(a["w_out"][0], 256)
    o["w_route"] = np.ascontiguousarray(np.concatenate(
        [a["w_r1"][0], a["w_r2"][0].transpose(1, 0, 2).reshape(D, 32)], 1).reshape(KD, P, 36).transpose(1, 0, 2))
    o["b_route"] = np.concatenate([a["b_r1"][0], a["b_r2"][0].reshape(32)])[None, :]
    for n in ("gate", "up"):
        o[f"w_{n}"] = np.ascontiguousarray(a[f"w_{n}"][0].reshape(N_EXP, KD, P, 256).transpose(0, 2, 1, 3).reshape(N_EXP, P, -1))
    o["w_down"] = np.ascontiguousarray(a["w_down"][0].reshape(N_EXP, 2, P, D).transpose(0, 2, 1, 3).reshape(N_EXP, P, -1))
    ple = np.concatenate([a["w_ple_gate"][0], a["w_ple"][0]], 0)
    o["w_ple"] = panels(ple, P)
    r = np.arange(P)
    o["ident"] = np.eye(P, dtype=np.float32)
    o["masks"] = np.ascontiguousarray(np.stack([
        np.where(r[None, :] <= r[:, None], 0, NEG),
        np.where(r[:, None] < r[None, :], 0, NEG),
        r[:, None] < r[None, :],
        r[:, None] >= r[None, :]], 1).astype(np.float32))
    vecs = dict(attn_norm=a["attn_norm"][0], ffn_norm=a["ffn_norm"][0], ple_norm=a["ple_norm"][0],
                final_norm=a["final_norm"], kv_norm=a["kv_norm"][0],
                norm1_0=a["norm1_w_2"][0], norm1_1=a["norm1_w_2"][1], norm2_0=a["norm2_w_2"][0],
                norm2_1=a["norm2_w_2"][1], q_norm=a["mla_q_norm_w_2"][0], mkv_norm=a["mla_kv_norm_w_2"][0],
                qn=a["mla_qn_w_2"][0], qr=a["mla_qr_w_2"][0], kn=a["mla_kn_w_2"][0], kr=a["mla_kr_w_2"][0],
                o_norm=a["hg_o_norm_w_2"][0], b_ada_0=a["ada_b_2"][0], b_ada_1=a["ada_b_2"][1],
                lb0_f=a["hg_lb_logits_2"][0, 0], lb0_b=a["hg_lb_logits_2"][0, 1],
                lb1_f=a["hg_lb_logits_2"][1, 0], lb1_b=a["hg_lb_logits_2"][1, 1],
                c_lat=a["c_2"][0], c_ctx=a["c_ctx_2"])
    vec = np.zeros((P, VEC_COLS), np.float32)
    for n, (at, cols) in VEC_AT.items():
        v = vecs[n]
        rows = min(P, v.size)
        vec[0:rows, at:at + cols] = v.reshape(cols, rows).T
    o["vec"] = vec
    for i in range(2):
        o[f"ada_{i}"] = panels(a["ada_w_2"][i], 256)
        w13 = np.stack([a["ffn_w1_2"][i].reshape(D, KF, P), a["ffn_w3_2"][i].reshape(D, KF, P)], 2)
        o[f"w13_{i}"] = panels(w13.reshape(D, 2 * D_FF), 256)
        w2 = a["ffn_w2_2"][i].reshape(2, HALF * P, D)
        o[f"w2_{i}"] = np.concatenate([panels(w2[0], P), panels(w2[1], P)])
    mla_in = a["mla_w_in_2"][0]
    o["mla_in"] = panels(np.concatenate([mla_in, mla_in[:, 640:]], 1), P)
    uq = a["mla_w_uq_2"][0].reshape(384, HEADS, 192)
    o["mla_uq"] = panels(np.concatenate([uq, uq[:, :, P:]], 2).reshape(384, HEADS * 256), 256)
    o["mla_ukv"] = panels(a["mla_w_ukv_2"][0], 256)
    o["mla_out"] = panels(a["mla_w_o_2"][0], 256)
    o["rope"], o["rot"] = rope_tables()
    hg = a["hg_w_in_2"][0]
    part = [hg[:, n * D:(n + 1) * D] for n in range(5)]
    o["hg_in"] = panels(np.concatenate([part[n] for n in (1, 2, 0, 4, 3)], 1), P)
    o["hg_out"] = panels(a["hg_w_o_2"][0], 256)
    o["levels"] = level_masks()
    return o


OPTIONS = {}


def kernel(**inputs):
    import concourse.bacc as _bacc
    from concourse.bass_utils import run_bass_kernel_spmd as _run

    nc = _bacc.Bacc("TRN2", target_bir_lowering=False, num_devices=1)
    arrays, dram = {}, {}
    for name, a in arrange(inputs).items():
        arrays[f"in_{name}_dram"] = a
        dram[name] = nc.dram_tensor(f"in_{name}_dram", a.shape, mybir.dt.from_np(a.dtype), kind="ExternalInput").ap()
    skew = nc.dram_tensor("bias_skew", (HEADS, P * (SKEW + 1)), F32).ap()
    dram["skew_flat"] = skew
    dram["skew"] = skew.rearrange("h (p n) -> h p n", p=P)
    dram["comb"] = nc.dram_tensor("expert_comb", (N_EXP, T), F32).ap()
    out = nc.dram_tensor("out_0_dram", (P, KD, T), F32, kind="ExternalOutput").ap()
    program(nc, dram, out, **OPTIONS)
    r = _run(nc, [arrays], core_ids=[0])
    got = np.asarray(r.results[0]["out_0_dram"])
    return np.ascontiguousarray(got.transpose(2, 1, 0).reshape(1, T, D))
```
